# Optimizing a Trainium2 kernel written in Bass

```python
import jax, jax.numpy as jnp
from jax import lax
import numpy as np

D_MODEL = 1024
BATCH = 1
SEQ = 512
DEPTH = 2

ATTN_Q_HEADS = 8
ATTN_KV_HEADS = 2
ATTN_HEAD_DIM = 64
ATTN_GROUP = ATTN_Q_HEADS // ATTN_KV_HEADS
WINDOW = 128
ATTN_BLOCK = 128
ROPE_THETA = 500000.0
ROPE_DIM = ATTN_HEAD_DIM // 4

RET_HEADS = 4
RET_QK_DIM = 64
RET_V_DIM = 128
RET_CHUNK = 128
RET_ROPE_THETA = 10000.0

CONV_CH = 512
CONV_WIDTH = 3

N_BRANCH = 3
BRANCH_W = 512

D_FF = ((8 * D_MODEL // 3 + 255) // 256) * 256

EPS = 1e-6

COL_SIZES = [
    ATTN_Q_HEADS * ATTN_HEAD_DIM,
    ATTN_KV_HEADS * ATTN_HEAD_DIM,
    ATTN_KV_HEADS * ATTN_HEAD_DIM,
    RET_HEADS * RET_QK_DIM,
    RET_HEADS * RET_QK_DIM,
    RET_HEADS * RET_V_DIM,
    RET_HEADS * RET_V_DIM,
    CONV_CH,
    CONV_CH,
    CONV_CH,
    N_BRANCH * D_MODEL,
]
D_IN = int(sum(COL_SIZES))
SPLIT_POINTS = [int(v) for v in np.cumsum(COL_SIZES)[:-1]]

kernel_name = "hybrid_swa_retention_shortconv_gated_block"

def rms_norm(x, g):
    x32 = x.astype(jnp.float32)
    y = x32 * lax.rsqrt(jnp.mean(x32 * x32, axis=-1, keepdims=True) + EPS)
    return (y * g.astype(jnp.float32)).astype(x.dtype)

def rotary(x, rot_dim, theta):
    seq = x.shape[1]
    half = rot_dim // 2
    inv = theta ** (-jnp.arange(half, dtype=jnp.float32) / half)
    ang = jnp.arange(seq, dtype=jnp.float32)[:, None] * inv[None, :]
    cos = jnp.cos(ang)[None, :, None, :]
    sin = jnp.sin(ang)[None, :, None, :]
    xr = x[..., :rot_dim].astype(jnp.float32)
    x1, x2 = xr[..., :half], xr[..., half:]
    rot = jnp.concatenate([x1 * cos - x2 * sin, x2 * cos + x1 * sin], axis=-1)
    return jnp.concatenate([rot.astype(x.dtype), x[..., rot_dim:]], axis=-1)

def swa_attention(q, k, v, sinks):
    b, s, _ = q.shape
    nb = s // ATTN_BLOCK
    dt = q.dtype
    q = rotary(q.reshape(b, s, ATTN_Q_HEADS, ATTN_HEAD_DIM), ROPE_DIM, ROPE_THETA)
    k = rotary(k.reshape(b, s, ATTN_KV_HEADS, ATTN_HEAD_DIM), ROPE_DIM, ROPE_THETA)
    v = v.reshape(b, s, ATTN_KV_HEADS, ATTN_HEAD_DIM)
    qb = (q.astype(jnp.float32) * ATTN_HEAD_DIM ** -0.5).reshape(
        b, nb, ATTN_BLOCK, ATTN_KV_HEADS, ATTN_GROUP, ATTN_HEAD_DIM)
    pad = ((0, 0), (ATTN_BLOCK, 0), (0, 0), (0, 0))
    kp = jnp.pad(k, pad).astype(jnp.float32).reshape(b, nb + 1, ATTN_BLOCK, ATTN_KV_HEADS, ATTN_HEAD_DIM)
    vp = jnp.pad(v, pad).astype(jnp.float32).reshape(b, nb + 1, ATTN_BLOCK, ATTN_KV_HEADS, ATTN_HEAD_DIM)
    kw = jnp.concatenate([kp[:, :-1], kp[:, 1:]], axis=2)
    vw = jnp.concatenate([vp[:, :-1], vp[:, 1:]], axis=2)
    qi = jnp.arange(ATTN_BLOCK)[:, None]
    kj = jnp.arange(2 * ATTN_BLOCK)[None, :]
    diff = ATTN_BLOCK + qi - kj
    n_idx = jnp.arange(nb)[:, None, None]
    kpos = (n_idx - 1) * ATTN_BLOCK + kj[None]
    mask = (diff[None] >= 0) & (diff[None] < WINDOW) & (kpos >= 0)
    scores = jnp.einsum('bnqhgd,bnkhd->bnhgqk', qb, kw)
    scores = jnp.where(mask[None, :, None, None], scores, -jnp.inf)
    sink = sinks.astype(jnp.float32).reshape(1, 1, ATTN_KV_HEADS, ATTN_GROUP, 1, 1)
    m = jnp.maximum(jnp.max(scores, axis=-1, keepdims=True), sink)
    p = jnp.exp(scores - m)
    denom = jnp.sum(p, axis=-1, keepdims=True) + jnp.exp(sink - m)
    p = p / denom
    out = jnp.einsum('bnhgqk,bnkhd->bnqhgd', p, vw)
    return out.reshape(b, s, ATTN_Q_HEADS * ATTN_HEAD_DIM).astype(dt)

def retention(q, k, v, g):
    b, s, _ = q.shape
    nc = s // RET_CHUNK
    dt = q.dtype
    q = rotary(q.reshape(b, s, RET_HEADS, RET_QK_DIM), RET_QK_DIM, RET_ROPE_THETA)
    k = rotary(k.reshape(b, s, RET_HEADS, RET_QK_DIM), RET_QK_DIM, RET_ROPE_THETA)
    qc = q.astype(jnp.float32).reshape(b, nc, RET_CHUNK, RET_HEADS, RET_QK_DIM)
    kc = (k.astype(jnp.float32) * RET_QK_DIM ** -0.5).reshape(b, nc, RET_CHUNK, RET_HEADS, RET_QK_DIM)
    vc = v.astype(jnp.float32).reshape(b, nc, RET_CHUNK, RET_HEADS, RET_V_DIM)
    log_gamma = jnp.log1p(-jnp.exp2(-(5.0 + jnp.arange(RET_HEADS, dtype=jnp.float32))))
    idx = jnp.arange(RET_CHUNK, dtype=jnp.float32)
    rel = idx[:, None] - idx[None, :]
    dmask = jnp.exp(jnp.where(rel[None] >= 0, log_gamma[:, None, None] * rel[None], -jnp.inf))
    att = jnp.einsum('bnqhd,bnkhd->bnhqk', qc, kc) * dmask[None, None]
    inner = jnp.einsum('bnhqk,bnkhe->bnqhe', att, vc)
    zeta = jnp.exp(log_gamma[:, None] * (RET_CHUNK - 1.0 - idx)[None])
    xi = jnp.exp(log_gamma[:, None] * (idx + 1.0)[None])
    chunk_decay = jnp.exp(log_gamma * RET_CHUNK)[None, :, None, None]
    kv = jnp.einsum('bnkhd,hk,bnkhe->nbhde', kc, zeta, vc)

    def step(state, kv_n):
        return chunk_decay * state + kv_n, state

    _, state_prev = lax.scan(step, jnp.zeros((b, RET_HEADS, RET_QK_DIM, RET_V_DIM), jnp.float32), kv)
    cross = jnp.einsum('bnqhd,hq,nbhde->bnqhe', qc, xi, state_prev)
    y = (inner + cross).reshape(b, s, RET_HEADS, RET_V_DIM)
    y = y * lax.rsqrt(jnp.mean(y * y, axis=-1, keepdims=True) + EPS)
    out = jax.nn.silu(g.reshape(b, s, RET_HEADS, RET_V_DIM).astype(jnp.float32)) * y
    return out.reshape(b, s, RET_HEADS * RET_V_DIM).astype(dt)

def short_conv(gate_b, gate_c, xv, w):
    u = gate_c * xv
    y = lax.conv_general_dilated(
        u, w.astype(u.dtype)[:, None, :], window_strides=(1,),
        padding=[(CONV_WIDTH - 1, 0)], dimension_numbers=('NWC', 'WIO', 'NWC'),
        feature_group_count=CONV_CH)
    return gate_b * y

def token_mixer(u, w_in_l, sinks_l, conv_w_l, w_branch_l, b_gate_l, w_out_l):
    b, s, _ = u.shape
    proj = u @ w_in_l
    (aq, ak, av, rq, rk, rv, rg, cb, cc, cx, gates) = jnp.split(proj, SPLIT_POINTS, axis=-1)
    ya = swa_attention(aq, ak, av, sinks_l)
    yr = retention(rq, rk, rv, rg)
    yc = short_conv(cb, cc, cx, conv_w_l)
    branches = jnp.stack([ya, yr, yc], axis=-2)
    branch_out = jnp.einsum('bsnc,ncd->bsnd', branches, w_branch_l)
    g = jax.nn.sigmoid(gates.reshape(b, s, N_BRANCH, D_MODEL) + b_gate_l)
    merged = jnp.sum(g * branch_out, axis=-2)
    return merged @ w_out_l

def swiglu(u, wg, wu, wd):
    return (jax.nn.silu(u @ wg) * (u @ wu)) @ wd

def setup_inputs(seed: int = 0) -> dict:
    key = jax.random.key(seed)
    ks = jax.random.split(key, 14)
    f32 = jnp.float32
    nrm = lambda k, shp, sc: jax.random.normal(k, shp, f32) * sc
    return {
        "x": nrm(ks[0], (BATCH, SEQ, D_MODEL), 1.0),
        "norm_mix": 1.0 + nrm(ks[1], (DEPTH, D_MODEL), 0.02),
        "w_in": nrm(ks[2], (DEPTH, D_MODEL, D_IN), D_MODEL ** -0.5),
        "attn_sinks": nrm(ks[3], (DEPTH, ATTN_Q_HEADS), 0.5),
        "conv_w": nrm(ks[4], (DEPTH, CONV_WIDTH, CONV_CH), CONV_WIDTH ** -0.5),
        "w_branch": nrm(ks[5], (DEPTH, N_BRANCH, BRANCH_W, D_MODEL), BRANCH_W ** -0.5),
        "b_gate": nrm(ks[6], (DEPTH, N_BRANCH, D_MODEL), 0.1),
        "w_out": nrm(ks[7], (DEPTH, D_MODEL, D_MODEL), D_MODEL ** -0.5),
        "norm_ffn": 1.0 + nrm(ks[8], (DEPTH, D_MODEL), 0.02),
        "w_ffn_gate": nrm(ks[9], (DEPTH, D_MODEL, D_FF), D_MODEL ** -0.5),
        "w_ffn_up": nrm(ks[10], (DEPTH, D_MODEL, D_FF), D_MODEL ** -0.5),
        "w_ffn_down": nrm(ks[11], (DEPTH, D_FF, D_MODEL), D_FF ** -0.5),
        "norm_final": 1.0 + nrm(ks[12], (D_MODEL,), 0.02),
    }

def reference(x, norm_mix, w_in, attn_sinks, conv_w, w_branch, b_gate, w_out,
              norm_ffn, w_ffn_gate, w_ffn_up, w_ffn_down, norm_final):
    h = x
    for layer in range(DEPTH):
        u = rms_norm(h, norm_mix[layer])
        h = h + token_mixer(u, w_in[layer], attn_sinks[layer], conv_w[layer],
                            w_branch[layer], b_gate[layer], w_out[layer])
        u = rms_norm(h, norm_ffn[layer])
        h = h + swiglu(u, w_ffn_gate[layer], w_ffn_up[layer], w_ffn_down[layer])
    return rms_norm(h, norm_final)


_drawn_inputs = setup_inputs


def setup_inputs(seed=0):
    import zlib

    import numpy as np

    out = dict(_drawn_inputs(seed))
    spreads = {}
    factors = {'attn_sinks': 5.142, 'norm_ffn': 2.86, 'norm_final': 2.885}
    for name, (base, spread) in spreads.items():
        noise = np.random.default_rng([zlib.crc32(name.encode()), seed]).standard_normal(out[name].shape)
        drawn = base * np.exp(spread * noise) if base else spread * noise
        out[name] = __import__('jax').numpy.asarray(drawn.astype(out[name].dtype))
    for name, factor in factors.items():
        out[name] = (out[name] * factor).astype(out[name].dtype)
    return out
```

```python
from contextlib import ExitStack

import numpy as np
import concourse.bass as bass
from concourse import mybir
from concourse.bass import ds

F32 = mybir.dt.float32
F32R = mybir.dt.float32r
ALU = mybir.AluOpType
ACT = mybir.ActivationFunctionType
AXIS_X = mybir.AxisListType.X

P = 128
EPS = 1e-6
ROPE_THETA, RET_ROPE_THETA = 500000.0, 10000.0

HQ, HKV, DH, ROT = 8, 2, 64, 16
RH, RDK, RDV = 4, 64, 128
AQ, AK, AV, RQ, RK, RV, RG, TOKW = 0, 512, 640, 768, 1024, 1280, 1792, 2304
CB, CC, CX, GATES = 2304, 2816, 3328, 3840

C_ID = 0
C_MASK = C_ID + P
C_DMASK = C_MASK + 4 * 256
C_XI = C_DMASK + 4 * P
C_COSA = C_XI + 2 * P
C_SINA = C_COSA + 32
C_COSR = C_SINA + 32
C_SINR = C_COSR + 128
C_ZETA = C_SINR + 128
C_DECAY = C_ZETA + RH
C_ALL = C_DECAY + 2


def shape_constants(S):
    out = np.zeros((P, C_ALL), np.float32)
    NB = S // P
    out[:, C_ID:C_ID + P] = np.eye(P)
    qi, kj = np.arange(P)[:, None], np.arange(2 * P)[None]
    diff = P + qi - kj
    for b in range(4):
        keep = (diff >= 0) & (diff < P) & ((b - 1) * P + kj >= 0)
        out[:, C_MASK + 256 * b:C_MASK + 256 * (b + 1)] = np.where(keep, 0.0, -3.0e38)
    idx = np.arange(P, dtype=np.float64)
    gamma = 1.0 - np.exp2(-(5.0 + np.arange(RH)))
    for h in range(RH):
        par, j = h % 2, h // 2
        rel = idx[None] - idx[:, None]
        at = C_DMASK + (2 * par + j) * P
        out[:, at:at + P] = np.where(rel >= 0, gamma[h] ** np.maximum(rel, 0), 0.0) * RDK ** -0.5
        rows = slice(64 * par, 64 * par + 64)
        out[rows, C_XI + j * P:C_XI + (j + 1) * P] = gamma[h] ** (idx + 1)
        out[:, C_ZETA + h] = gamma[h] ** (P - 1 - idx) * RDK ** -0.5
        out[rows, C_DECAY + j] = gamma[h] ** P
    for half, theta, c_cos, c_sin in ((ROT // 2, ROPE_THETA, C_COSA, C_SINA),
                                      (RDK // 2, RET_ROPE_THETA, C_COSR, C_SINR)):
        inv = np.float32(theta) ** (-np.arange(half, dtype=np.float32) / np.float32(half))
        ang = (np.arange(S, dtype=np.float32)[:, None] * inv[None]).astype(np.float64)
        for b in range(NB):
            out[:, c_cos + b * half:c_cos + (b + 1) * half] = np.cos(ang[b * P:(b + 1) * P])
            out[:, c_sin + b * half:c_sin + (b + 1) * half] = np.sin(ang[b * P:(b + 1) * P])
    return out


def trunk(nc, x, norm_mix, w_in, attn_sinks, conv_w, w_branch, b_gate, w_out,
          norm_ffn, w_ffn_gate, w_ffn_up, w_ffn_down, norm_final, consts, out):
    _, S, D = x.shape
    L = w_in.shape[0]
    FF = w_ffn_gate.shape[2]
    NB, DC, FC = S // P, D // P, FF // P
    assert (NB, DC, FC, L) == (4, 8, 22, 2) and w_in.shape[2] == GATES + 3 * D

    SLOTS = 4
    LEAD = 16
    UNIT_A, UNIT_B, UNIT_C, UNIT_M, UNIT_O, UNIT_G, UNIT_D, UNITS = 0, 18, 34, 42, 66, 74, 118, 140
    TILE_A, TILE_B, TILE_C, TILE_M, TILE_O, TILE_G, TILE_D, TILES = 0, 20, 36, 48, 80, 88, 132, 140
    assert UNITS % SLOTS == 0 and TILES % 4 == 0
    HEAD = [0, 2, 4, 6, 1, 3, 5, 7]
    R_MIX, R_FFN, R_FIN, R_BG, R_CONV = 0, L * DC, 2 * L * DC, 2 * L * DC + DC, 2 * L * DC + DC + 3 * L * DC
    R_ALL = R_CONV + L * 12

    with ExitStack() as ctx:
        def sb(name, shape, dt=F32, at=ctx):
            return at.enter_context(nc.sbuf_tensor(name, shape, dt))

        def sem(name):
            return ctx.enter_context(nc.semaphore(name))

        h = sb("h", [P, DC, S])
        uh = sb("uh", [P, DC, S], F32R)
        ul = sb("ul", [P, DC, S], F32R)
        raw = sb("raw", [P, SLOTS, 1024])
        wh = sb("wh", [P, SLOTS, 1024], F32R)
        wl = sb("wl", [P, SLOTS, 1024], F32R)
        cst = sb("cst", [P, C_ALL])
        prm = sb("prm", [P, R_ALL])
        sinks = sb("sinks", [P, L * HQ])
        ones = sb("ones", [P, LEAD])
        epsc = sb("epsc", [P, 1])
        rms = sb("rms", [P, 2, NB])
        rb = sb("rb", [P, NB, P])
        with ExitStack() as one:
            tok = sb("tok", [P, NB, TOKW], at=one)
            bh = sb("bh", [P, 4, S], F32R, at=one)
            bl = sb("bl", [P, 4, S], F32R, at=one)
            sg = sb("sg", [P, 4, S], at=one)
            cbs = sb("cbs", [P, S], at=one)
            ccs = sb("ccs", [P, S], at=one)
            ub = sb("ub", [P, S + 2], at=one)
            blk = sb("blk", [P, 2048], at=one)
            tmp = sb("tmp", [P, 10 * ROT + 8 * RDK], at=one)
            qT = sb("qT", [P, 512], at=one)
            rT = sb("rT", [P, 512], at=one)
            kwin = sb("kwin", [P, 2, 256], at=one)
            att = sb("att", [P, 2, 2, P], at=one)
        with ExitStack() as two:
            fh = sb("fh", [P, FC, S], F32R, at=two)
            fl = sb("fl", [P, FC, S], F32R, at=two)
        size_one = 4 * (NB * TOKW + 3 * 4 * S + 2 * S + S + 2 + 2048 + 10 * ROT + 8 * RDK + 2048)
        region1 = sb("region1", [P, max(size_one, 8 * FC * S) // 4 + 8])
        with ExitStack() as one:
            S_sb = sb("S_sb", [P, 8, 256], at=one)
            PT = sb("PT", [P, 4, 4, P], at=one)
        with ExitStack() as two:
            m = sb("m", [P, DC, S], at=two)
        with ExitStack() as three:
            ut = sb("ut", [P, 2, S], at=three)
            sq = sb("sq", [P, 2, S], at=three)
            ssq = sb("ssq", [P, S], at=three)
            sgt = sb("sgt", [P, S], at=three)
            gp = sb("gp", [P, S], at=three)
            ft = sb("ft", [P, S], at=three)
        region2 = sb("region2", [P, DC * S])
        vprev = sb("vprev", [P, P])
        qx = sb("qx", [P, 2, P])
        state = sb("state", [P, RH, P])
        junk = sb("junk", [P, RH * P])
        prod = sb("prod", [P, S])
        mx, negm, sinkm, sums, rden = (sb(n, [P, 8]) for n in ("mx", "negm", "sinkm", "sums", "rden"))
        ssqR = sb("ssqR", [P, NB * RH])
        rstdR = sb("rstdR", [P, NB * RH])

        bank = [ctx.enter_context(nc.psum_tensor(f"bank{i}", [P, 512], F32)) for i in range(8)]

        tokf = tok[:].rearrange("p b c -> p (b c)")
        ident = cst[:, C_ID:C_ID + P]

        def tcols(b, c, n):
            return tokf[:, ds(b * TOKW + c, n)]

        x_tok = tokf[:, 0:NB * D].rearrange("p (b c) -> p b c", b=NB)
        y_fm = tokf[:, 0:DC * S].rearrange("p (c t) -> p c t", c=DC)
        y_tok = tokf[:, DC * S:DC * S + NB * D].rearrange("p (b c) -> p b c", b=NB)
        yfm = tok[:, :, RV:RV + 1024].rearrange("p c (w t) -> p w c t", w=2)

        x_in = sem("x_in")
        params_in = sem("params_in")
        consts_in = sem("consts_in")
        raw_full = [sem(f"raw_full{s}") for s in range(SLOTS)]
        split_done = sem("split_done")
        units_begun = sem("units_begun")
        tile_full = sem("tile_full")
        bank_free = [sem(f"bank_free{b}") for b in range(4)]
        x_turned = sem("x_turned")
        h_loaded = sem("h_loaded")
        params_turned = sem("params_turned")
        params_ready = sem("params_ready")
        sq_ready = sem("sq_ready")
        ssq_added = sem("ssq_added")
        ssq_cleared = sem("ssq_cleared")
        ms_ready = sem("ms_ready")
        std_ready = sem("std_ready")
        rb_ready = sem("rb_ready")
        rstd_ready = sem("rstd_ready")
        ut_ready = sem("ut_ready")
        uh_ready = sem("uh_ready")
        u_ready = sem("u_ready")
        rope_done = sem("rope_done")
        turned_qk = sem("turned_qk")
        taken_qk = sem("taken_qk")
        qx_ready = sem("qx_ready")
        scores_full = sem("scores_full")
        scores_taken = sem("scores_taken")
        max_ready = sem("max_ready")
        exp_done = sem("exp_done")
        ret_full = sem("ret_full")
        att_ready = sem("att_ready")
        y_full = sem("y_full")
        y_taken = sem("y_taken")
        state_ready = sem("state_ready")
        probs_turned = sem("probs_turned")
        probs_a = sem("probs_a")
        probs_v = sem("probs_v")
        pv_full = sem("pv_full")
        pv_taken = sem("pv_taken")
        conv_ready = sem("conv_ready")
        hi_ready = sem("hi_ready")
        branch_ready = sem("branch_ready")
        ret_std = sem("ret_std")
        ret_g = sem("ret_g")
        ret_sig = sem("ret_sig")
        ret_gated = sem("ret_gated")
        branch_turned = sem("branch_turned")
        branch_taken = sem("branch_taken")
        gate_ready = sem("gate_ready")
        m_ready = sem("m_ready")
        sig_ready = sem("sig_ready")
        fh_ready = sem("fh_ready")
        f_ready = sem("f_ready")
        final_ready = sem("final_ready")
        out_turned = sem("out_turned")
        out_ready = sem("out_ready")
        out_sent = sem("out_sent")

        def full(eng, t):
            eng.wait_ge(tile_full, t + 1)

        block = ctx.enter_context(nc.Block())

        @block.sync
        def _(sp):
            sp.dma_start(cst[:], consts).then_inc(consts_in, 16)
            sp.dma_start(sinks[:], attn_sinks.rearrange("(a l) h -> a (l h)", a=1).broadcast_to([P, L * HQ])).then_inc(consts_in, 16)

            def load(n, slot, src, k):
                sp.wait_ge(split_done, n + 1)
                sp.dma_start(raw[:, slot, :].rearrange("p (k n) -> p k n", k=k), src).then_inc(raw_full[slot], 16)

            def rows(w, lead, r0, nk, c0, nc_):
                return w[ds(lead, 1), ds(r0, nk * P), ds(c0, nc_)].rearrange("a (k p) n -> p (a k) n", p=P)

            wb = w_branch.rearrange("l i c d -> (l i) c d")

            with sp.Fori(0, L) as l:
                n0 = l * UNITS
                with sp.Fori(0, 4) as g:
                    for j in range(4):
                        load(n0 + g * 4 + j, j, rows(w_in, l, 2 * P * j, 2, g * 512, 512), 2)
                for j in range(2):
                    load(n0 + 16 + j, j, rows(w_in, l, 4 * P * j, 4, 2048, 256), 4)
                with sp.Fori(0, 4) as j:
                    for q, c0 in enumerate((CC, CX, CB, GATES + 2 * D)):
                        load(n0 + j * 4 + (UNIT_B + q), (UNIT_B + q) % SLOTS, rows(w_in, l, 0, 8, j * P + c0, P), 8)

                def gate_units(n, i, g, off):
                    for q in range(4):
                        load(n + q, (off + q) % SLOTS, rows(w_in, l, 0, 8, i * D + (GATES + (4 * g + q) * P), P), 8)

                def branch_units(n, i, g, off):
                    for q in range(2):
                        load(n + q, (off + q) % SLOTS, rows(wb, l * 3 + i, 0, 4, 512 * g + 256 * q, 256), 4)

                branch_units(n0 + UNIT_C, 2, 0, UNIT_C)
                gate_units(n0 + (UNIT_C + 2), 2, 1, UNIT_C + 2)
                branch_units(n0 + (UNIT_C + 6), 2, 1, UNIT_C + 6)
                with sp.Fori(0, 2) as i:
                    for g in range(2):
                        gate_units(n0 + i * 12 + (UNIT_M + 6 * g), i, g, UNIT_M + 6 * g)
                        branch_units(n0 + i * 12 + (UNIT_M + 6 * g + 4), i, g, UNIT_M + 6 * g + 4)
                with sp.Fori(0, 2) as i:
                    for q in range(4):
                        load(n0 + i * 4 + (UNIT_O + q), (UNIT_O + q) % SLOTS, rows(w_out, l, 0, 8, i * 512 + q * P, P), 8)
                with sp.Fori(0, FC // 2) as i:
                    for q in range(4):
                        w = w_ffn_up if q % 2 else w_ffn_gate
                        load(n0 + i * 4 + (UNIT_G + q), (UNIT_G + q) % SLOTS, rows(w, l, 0, 8, i * 256 + (q // 2) * P, P), 8)
                for half in range(2):
                    def down(j, n, off):
                        load(n0 + n, off % SLOTS, rows(w_ffn_down, l, j * 256, 2, 512 * half, 512), 2)
                    u0 = UNIT_D + 11 * half
                    down(0, u0, u0)
                    with sp.Fori(0, 2) as i:
                        for q in range(4):
                            down(i * 4 + (1 + q), i * 4 + (u0 + 1 + q), u0 + 1 + q)
                    down(9, u0 + 9, u0 + 9)
                    down(10, u0 + 10, u0 + 10)

            for b in range(NB):
                sp.wait_ge(out_ready, 2 * b + 2)
                sp.dma_start(out.rearrange("a (b p) d -> p (a b) d", p=P)[:, b, :], y_tok[:, b, :]).then_inc(out_sent, 16)
            sp.wait_ge(out_sent, 16 * NB)

        @block.gpsimd
        def _(pool):
            with pool.Fori(0, L * UNITS // SLOTS) as q:
                for s in range(SLOTS):
                    pool.wait_ge(raw_full[s], q * 16 + 16)
                    pool.wait_ge(units_begun, q * 4 + (s + 1))
                    pool.tensor_tensor(wh[:, s, 0:LEAD], raw[:, s, 0:LEAD], ones[:], ALU.mult)
                    pool.tensor_scalar(wh[:, s, LEAD:], raw[:, s, LEAD:], 1.0, 0.0, ALU.mult, ALU.add)
                    pool.drain()
                    pool.tensor_tensor(wl[:, s, :], raw[:, s, :], wh[:, s, :].bitcast(F32), ALU.subtract).then_inc(split_done, 1)

        @block.tensor
        def _(pe):
            def begin(n):
                pe.wait_ge(split_done, n + 1 + SLOTS)

            def may_write(t4, b):
                pe.wait_ge(bank_free[b], t4 + 1)

            def turn(dst, src):
                return pe.transpose(dst, src, ident)

            def feature_unit(n, slot, t4, b, xh, xl, nk, width=P, c0=0, first=True, waits=None):
                if first:
                    begin(n)
                may_write(t4, b)
                a = wh[:, slot, :].rearrange("p (k n) -> p k n", k=nk)
                r = wl[:, slot, :].rearrange("p (k n) -> p k n", k=nk)
                cols = slice(c0, c0 + P)
                for k in range(nk):
                    if waits is not None:
                        pe.wait_ge(*waits(k))
                    mm = pe.matmul(bank[b][:], a[:, k, cols], xh[:, k, :], start=k == 0, stop=False)
                    if first and k == 0:
                        mm.then_inc(units_begun, 1)
                    pe.matmul(bank[b][:], a[:, k, cols], xl[:, k, :], start=False, stop=False)
                    mm = pe.matmul(bank[b][:], r[:, k, cols], xh[:, k, :], start=False, stop=k == nk - 1)
                mm.then_inc(tile_full, 1)

            def token_product(b, k, slot, kk, width, nk, start, stop):
                a = wh[:, slot, :].rearrange("p (k n) -> p k n", k=nk)[:, kk, :]
                r = wl[:, slot, :].rearrange("p (k n) -> p k n", k=nk)[:, kk, :]
                t = slice(b * P, b * P + P)
                o = bank[b][:, 0:width]
                first = pe.matmul(o, uh[:, k, t], a, start=start, stop=False)
                pe.matmul(o, uh[:, k, t], r, start=False, stop=False)
                return first, pe.matmul(o, ul[:, k, t], a, start=False, stop=stop)

            def token_group(n, t4, units, nk, width, u0):
                for j in range(units):
                    begin(n + j)
                    last = j == units - 1
                    order = [(kk, b) for kk in range(nk) for b in range(NB)]
                    if last:
                        order = [(kk, b) for b in range(NB) for kk in range(nk)]
                    for at, (kk, b) in enumerate(order):
                        k = nk * j + kk
                        if u0 is not None:
                            pe.wait_ge(u_ready, u0 + k + 1)
                        if k == 0:
                            may_write(t4, b)
                        first, mm = token_product(b, k, j, kk, width, nk, k == 0, k == DC - 1)
                        if at == 0:
                            first.then_inc(units_begun, 1)
                        if k == DC - 1:
                            mm.then_inc(tile_full, 1)

            def norm(i):
                pe.wait_ge(ssq_added, i * 8 + 8)
                for b in range(NB):
                    mm = pe.matmul(bank[4][:, b:b + 1], ssq[:, b * P:b * P + P], ones[:, 0:1], start=True, stop=True)
                mm.then_inc(ms_ready, 1)
                pe.wait_ge(rb_ready, i + 1)
                for b in range(NB):
                    mm = turn(bank[5][:, b * P:b * P + P], rb[:, b, :])
                mm.then_inc(rstd_ready, 1)

            def block_turn(B):
                pe.wait_ge(rope_done, B + 1)
                for c in range(4):
                    mm = turn(bank[4][:, c * P:c * P + P], blk[:, c * P:c * P + P])
                mm.then_inc(turned_qk, 1)
                for c in range(4):
                    mm = turn(bank[5][:, c * P:c * P + P], blk[:, 768 + c * P:896 + c * P])
                mm.then_inc(turned_qk, 1)
                for c in range(2):
                    mm = turn(bank[6][:, c * P:c * P + P], blk[:, 512 + c * P:640 + c * P])
                mm.then_inc(turned_qk, 1)

            def block_scores(B):
                pe.wait_ge(taken_qk, B * 3 + 3)
                pe.wait_ge(pv_taken, B + 1)
                for i in range(4):
                    for s in range(2):
                        hd = HEAD[2 * i + s]
                        rows_ = slice(64 * (hd % 2), 64 * (hd % 2) + 64)
                        mm = pe.matmul(bank[4 + i][:, 256 * s:256 * s + 256], qT[rows_, (hd // 2) * P:(hd // 2) * P + P],
                                       kwin[rows_, hd // 4, :], start=True, stop=True)
                    mm.then_inc(scores_full, 1)

            def block_ret(b, B):
                pe.wait_ge(scores_taken, B * 4 + 4)
                for par in range(2):
                    rows_ = slice(64 * par, 64 * par + 64)
                    for j in range(2):
                        mm = pe.matmul(bank[7 - par][:, j * P:j * P + P], rT[rows_, (2 + j) * P:(3 + j) * P],
                                       rT[rows_, j * P:j * P + P], start=True, stop=True)
                    mm.then_inc(ret_full, 1)
                for hd in range(RH):
                    par, j = hd % 2, hd // 2
                    mm = pe.matmul(bank[5][64 * par:64 * par + 64, j * P:j * P + P], blk[:, 1280 + 64 * hd:1344 + 64 * hd],
                                   blk[:, 1536 + hd * P:1664 + hd * P], start=True, stop=True)
                mm.then_inc(ret_full, 1)

            def block_ret_out(l, b, B):
                pe.wait_ge(att_ready, B * 2 + 2)
                pe.wait_ge(qx_ready, B + 1)
                pe.wait_ge(state_ready, l * (NB + 1) + b + 1)
                for hd in range(RH):
                    par, j = hd % 2, hd // 2
                    o = bank[4][:, hd * P:hd * P + P]
                    pe.matmul(o, att[:, par, j, :], blk[:, 1536 + hd * P:1664 + hd * P], start=True, stop=False)
                    mm = pe.matmul(o, qx[:, j, :], state[:, hd, :], start=False, stop=True)
                mm.then_inc(y_full, 1)

            def block_probs(l, b, B):
                for s in range(8):
                    pe.wait_ge(exp_done, B * 9 + (s + 1))
                    if s == 4:
                        pe.wait_ge(state_ready, l * (NB + 1) + b + 2)
                        pe.wait_ge(y_taken, B + 1)
                    for c in range(2):
                        bk = 7 - c if s < 4 else 5 - c
                        mm = turn(bank[bk][:, (s % 4) * P:(s % 4) * P + P], S_sb[:, s, c * P:c * P + P])
                        if s % 4 == 3:
                            mm.then_inc(probs_turned, 1)

            def block_pv(b, B):
                pe.wait_ge(probs_a, B * 2 + 2)
                pe.wait_ge(probs_v, B * 2 + 2)
                for s in range(8):
                    hd = HEAD[s]
                    kv = hd // 4
                    o = bank[7][:, hd * DH:hd * DH + DH]
                    pe.matmul(o, PT[:, 2 * (s // 4), s % 4, :], vprev[:, kv * DH:kv * DH + DH], start=True, stop=False)
                    mm = pe.matmul(o, PT[:, 2 * (s // 4) + 1, s % 4, :], tcols(b, AV + kv * DH, DH), start=False, stop=True)
                mm.then_inc(pv_full, 1)

            def turn_branch(c0, n0, free):
                for c in range(4):
                    pe.wait_ge(*free(c))
                    for b in range(NB):
                        mm = turn(bank[4 + c][:, b * P:b * P + P], tok[:, b, c0 + c * P:c0 + c * P + P])
                    mm.then_inc(branch_turned, 1)

            pe.wait_ge(consts_in, 32)
            pe.wait_ge(params_in, 16 * 5)
            pe.transpose(bank[7][:, 0:R_ALL], blk[0:R_ALL, 0:P], cst[0:R_ALL, C_ID:C_ID + R_ALL]).then_inc(params_turned, 1)
            for c in range(DC):
                for b in range(NB):
                    if c == 0:
                        pe.wait_ge(x_in, 16 * NB)
                    if c == 7 and b == 0:
                        pe.wait_ge(params_ready, 1)
                    mm = turn(bank[c][:, b * P:b * P + P], x_tok[:, b, c * P:c * P + P])
                mm.then_inc(x_turned, 1)

            with pe.Fori(0, L) as l:
                n0 = l * UNITS
                q0 = l * (TILES // 4)
                norm(l * 2)
                with pe.Fori(0, 4) as g:
                    token_group(n0 + g * 4, q0 + g, 4, 2, 512, l * 24)
                token_group(n0 + 16, q0 + 4, 2, 4, 256, None)

                with pe.Fori(0, NB) as b:
                    B = l * NB + b
                    n = n0 + b * 4
                    qb = q0 + b + TILE_B // 4

                    def conv_unit(q):
                        feature_unit(n + (UNIT_B + q), (UNIT_B + q) % SLOTS, qb, q, uh, ul, 8)

                    block_turn(B)
                    conv_unit(0)
                    block_scores(B)
                    conv_unit(1)
                    block_ret(b, B)
                    conv_unit(2)
                    block_ret_out(l, b, B)
                    block_probs(l, b, B)
                    conv_unit(3)
                    block_pv(b, B)

                def gates(n, t4, off):
                    for q in range(4):
                        feature_unit(n + q, (off + q) % SLOTS, t4, q, uh, ul, 8)

                def branch(n, t4, off, ready0=None):
                    for q in range(2):
                        for e in range(2):
                            waits = None
                            if ready0 is not None and q == 0 and e == 0:
                                waits = lambda k: (branch_ready, ready0 + k + 1)
                            feature_unit(n + q, (off + q) % SLOTS, t4, 2 * q + e, bh, bl, 4, 256, P * e, e == 0, waits)

                branch(n0 + UNIT_C, q0 + TILE_C // 4, UNIT_C, l * 12)
                turn_branch(AQ, l * 8, lambda c: (pv_taken, l * NB + (NB + 1)))
                gates(n0 + (UNIT_C + 2), q0 + (TILE_C // 4 + 1), UNIT_C + 2)
                branch(n0 + (UNIT_C + 6), q0 + (TILE_C // 4 + 2), UNIT_C + 6)
                pe.wait_ge(ret_gated, l + 1)
                turn_branch(RQ, l * 8 + 4, lambda c: (branch_taken, l * 8 + c + 1))
                with pe.Fori(0, 2) as i:
                    for g in range(2):
                        o = UNIT_M + 6 * g
                        gates(n0 + i * 12 + o, q0 + i * 4 + (TILE_M // 4 + 2 * g), o)
                        branch(n0 + i * 12 + (o + 4), q0 + i * 4 + (TILE_M // 4 + 2 * g + 1), o + 4,
                               l * 12 + i * 4 + 4 if g == 0 else None)
                with pe.Fori(0, 2) as i:
                    for q in range(4):
                        waits = (lambda k: (u_ready, l * 24 + (8 + k + 1))) if q == 0 else None
                        feature_unit(n0 + i * 4 + (UNIT_O + q), (UNIT_O + q) % SLOTS, q0 + i + TILE_O // 4, q, uh, ul, 8,
                                     waits=waits)
                norm(l * 2 + 1)
                with pe.Fori(0, FC // 2) as i:
                    for q in range(4):
                        waits = (lambda k: (u_ready, l * 24 + (16 + k + 1))) if q == 0 else None
                        feature_unit(n0 + i * 4 + (UNIT_G + q), (UNIT_G + q) % SLOTS, q0 + i + TILE_G // 4, q, uh, ul, 8,
                                     waits=waits)

                for half in range(2):
                    u0 = UNIT_D + 11 * half
                    t4 = q0 + (TILE_D // 4 + half)

                    def down(j, n, off, start=False, last=False):
                        slot = off % SLOTS
                        begin(n0 + n)
                        a = wh[:, slot, :].rearrange("p (k n) -> p k n", k=2)
                        r = wl[:, slot, :].rearrange("p (k n) -> p k n", k=2)
                        order = [(kk, c) for kk in range(2) for c in range(4)]
                        if last:
                            order = [(kk, c) for c in range(4) for kk in range(2)]
                        for at, (kk, c) in enumerate(order):
                            if half == 0:
                                pe.wait_ge(f_ready, l * FC + j * 2 + (kk + 1))
                            if start and kk == 0:
                                may_write(t4, c)
                            xh, xl = fh[:, ds(j * 2 + kk, 1), :], fl[:, ds(j * 2 + kk, 1), :]
                            xh, xl = (v.rearrange("p a t -> p (a t)") for v in (xh, xl))
                            cols = slice(c * P, c * P + P)
                            mm = pe.matmul(bank[c][:], a[:, kk, cols], xh, start=start and kk == 0, stop=False)
                            if at == 0:
                                mm.then_inc(units_begun, 1)
                            pe.matmul(bank[c][:], a[:, kk, cols], xl, start=False, stop=False)
                            mm = pe.matmul(bank[c][:], r[:, kk, cols], xh, start=False, stop=last and kk == 1)
                            if last and kk == 1:
                                mm.then_inc(tile_full, 1)

                    down(0, u0, u0, start=True)
                    with pe.Fori(0, 2) as i:
                        for q in range(4):
                            down(i * 4 + (1 + q), i * 4 + (u0 + 1 + q), u0 + 1 + q)
                    down(9, u0 + 9, u0 + 9)
                    down(10, u0 + 10, u0 + 10, last=True)

            norm(2 * L)
            for c in range(4):
                may_write(L * (TILES // 4), c)
            for b in range(NB):
                for half in range(2):
                    if b == 0:
                        pe.wait_ge(final_ready, 4 * half + 4)
                    n = 2 * b + half
                    for c in range(4):
                        mm = turn(bank[n][:, c * P:c * P + P], y_fm[:, 4 * half + c, b * P:b * P + P])
                    mm.then_inc(out_turned, 1)

        @block.scalar
        def _(act):
            for b in range(NB):
                act.dma_start(x_tok[:, b, :], x.rearrange("a (b p) d -> p (a b) d", p=P)[:, b, :]).then_inc(x_in, 16)
            for r0, src in ((R_MIX, norm_mix.rearrange("l (c p) -> (l c) p", p=P)),
                            (R_FFN, norm_ffn.rearrange("l (c p) -> (l c) p", p=P)),
                            (R_FIN, norm_final.rearrange("(c p) -> c p", p=P)),
                            (R_BG, b_gate.rearrange("l i (c p) -> (l i c) p", p=P)),
                            (R_CONV, conv_w.rearrange("l i (c p) -> (l i c) p", p=P))):
                act.dma_start(blk[r0:r0 + src.shape[0], 0:P], src).then_inc(params_in, 16)

            def copy(dst, src):
                return act.activation(dst, src, ACT.Copy)

            def square(i8, c, par):
                if i8 is not None:
                    act.wait_ge(ssq_added, i8 - 1)
                act.activation(sq[:, par, :], h[:, ds(c, 1), :].rearrange("p a t -> p (a t)"), ACT.Square).then_inc(sq_ready, 1)

            def norm(i):
                act.wait_ge(ms_ready, i + 1)
                act.activation(rms[:, 0, :], bank[4][:, 0:NB], ACT.Sqrt, bias=epsc[:], scale=1.0 / D).then_inc(std_ready, 1)

            def round_u(i8):
                for c in range(DC):
                    act.wait_ge(ut_ready, i8 + (c + 1))
                    copy(uh[:, c, :], ut[:, c % 2, :]).then_inc(uh_ready, 1)

            act.wait_ge(params_turned, 1)
            copy(prm[:], bank[7][:, 0:R_ALL]).then_inc(params_ready, 1)
            for c in range(DC):
                act.wait_ge(h_loaded, c + 1)
                square(c if c >= 2 else None, c, c % 2)

            with act.Fori(0, L) as l:
                t0 = l * TILES
                q0 = l * (TILES // 4)
                norm(l * 2)
                round_u(l * 16)
                with act.Fori(0, 4) as g:
                    for b in range(NB):
                        full(act, t0 + g * 4 + b)
                        copy(tokf[:, ds(g * 512 + b * TOKW, 512)], bank[b][:]).then_inc(bank_free[b], 1)
                for b in range(NB):
                    full(act, t0 + (16 + b))
                    copy(tok[:, b, 2048:TOKW], bank[b][:, 0:256]).then_inc(bank_free[b], 1)

                with act.Fori(0, NB) as b:
                    B = l * NB + b
                    t = t0 + b * 4 + TILE_B
                    act.wait_ge(turned_qk, B * 3 + 1)
                    copy(qT[:], bank[4][:]).then_inc(taken_qk, 1)
                    copy(kwin[:, :, 0:P], kwin[:, :, P:2 * P])
                    act.wait_ge(turned_qk, B * 3 + 2)
                    copy(rT[:], bank[5][:]).then_inc(taken_qk, 1)
                    act.drain()
                    act.wait_ge(turned_qk, B * 3 + 3)
                    copy(kwin[:, :, P:2 * P], bank[6][:, 0:256].rearrange("p (a t) -> p a t", a=2)).then_inc(taken_qk, 1)
                    full(act, t)
                    act.wait_ge(pv_taken, B + 1)
                    copy(ccs[:], bank[0][:]).then_inc(bank_free[0], 1)
                    act.wait_ge(max_ready, B + 1)
                    for s in range(8):
                        act.activation(S_sb[:, s, :], S_sb[:, s, :], ACT.Exp, bias=negm[:, s:s + 1],
                                       accum_out=sums[:, s:s + 1]).then_inc(exp_done, 1)
                    act.activation(sinkm[:], sinkm[:], ACT.Exp).then_inc(exp_done, 1)
                    full(act, t + 2)
                    copy(cbs[:], bank[2][:]).then_inc(bank_free[2], 1)
                    act.wait_ge(y_full, B + 1)
                    for hd in range(RH):
                        act.activation(junk[:, hd * P:hd * P + P], bank[4][:, hd * P:hd * P + P], ACT.Square,
                                       accum_out=ssqR[:, ds(b * RH + hd, 1)])
                    copy(tcols(b, RQ, 512), bank[4][:]).then_inc(y_taken, 1)
                    act.wait_ge(probs_turned, B * 4 + 1)
                    copy(PT[:, 0, :, :], bank[7][:].rearrange("p (a t) -> p a t", a=4)).then_inc(probs_a, 1)
                    act.wait_ge(probs_turned, B * 4 + 3)
                    copy(PT[:, 2, :, :], bank[5][:].rearrange("p (a t) -> p a t", a=4)).then_inc(probs_a, 1)
                    act.wait_ge(conv_ready, B + 1)
                    copy(bh[:, ds(b, 1), :].rearrange("p a t -> p (a t)"), ccs[:]).then_inc(hi_ready, 1)
                    full(act, t + 3)
                    act.activation(sg[:, ds(b, 1), :].rearrange("p a t -> p (a t)"), bank[3][:], ACT.Identity,
                                   bias=prm[:, ds(l * 24 + b + (R_BG + 16), 1)]).then_inc(bank_free[3], 1)

                act.drain()
                act.activation(rstdR[:], ssqR[:], ACT.Sqrt, bias=epsc[:], scale=1.0 / RDV).then_inc(ret_std, 1)
                act.activation(sg[:], sg[:], ACT.Sigmoid).then_inc(gate_ready, 1)
                for c in range(4):
                    act.wait_ge(branch_turned, l * 8 + (c + 1))
                    copy(yfm[:, 0, c, :], bank[4 + c][:]).then_inc(branch_taken, 1)
                act.wait_ge(ret_g, l + 1)
                act.activation(tok[:, :, RG:TOKW], tok[:, :, RG:TOKW], ACT.Sigmoid).then_inc(ret_sig, 1)

                def gates(t, g4, i, g):
                    for q in range(4):
                        act.wait_ge(bank_free[q], g4 + 1)
                        full(act, t + q)
                        act.activation(sg[:, q, :], bank[q][:], ACT.Sigmoid,
                                       bias=prm[:, ds(l * 24 + i * 8 + (R_BG + 4 * g + q), 1)]).then_inc(bank_free[q], 1)

                gates(t0 + (TILE_C + 4), q0 + (TILE_C // 4 + 1), 2, 1)
                for c in range(4):
                    act.wait_ge(branch_turned, l * 8 + (c + 5))
                    copy(yfm[:, 1, c, :], bank[4 + c][:]).then_inc(branch_taken, 1)
                act.drain()
                with act.Fori(0, 2) as i:
                    full(act, t0 + i * 16 + (TILE_M - 1))
                    for c in range(4):
                        src = tokf[:, ds(i * 512 + (c * TOKW + RV), 512)]
                        copy(bh[:, c, :], src).then_inc(hi_ready, 1)
                    for g in range(2):
                        gates(t0 + i * 16 + (TILE_M + 8 * g), q0 + i * 4 + (TILE_M // 4 + 2 * g), i, g)
                for c in range(DC):
                    act.wait_ge(m_ready, l * 16 + (8 + c + 1))
                    copy(uh[:, c, :], m[:, c, :]).then_inc(uh_ready, 1)
                with act.Fori(0, 2) as i:
                    for q in range(4):
                        act.wait_ge(bank_free[q], q0 + i + (TILE_O // 4 + 2))
                        square(l * 16 + i * 4 + (8 + q), i * 4 + q, q % 2)
                norm(l * 2 + 1)
                round_u(l * 16 + 8)
                with act.Fori(0, FC // 2) as i:
                    t = t0 + i * 4 + TILE_G
                    for q in range(2):
                        full(act, t + 2 * q)
                        act.activation(sgt[:], bank[2 * q][:], ACT.Sigmoid).then_inc(sig_ready, 1)
                        act.wait_ge(bank_free[2 * q + 1], q0 + i + (TILE_G // 4 + 2))
                        copy(fh[:, ds(i * 2 + q, 1), :].rearrange("p a t -> p (a t)"), ft[:]).then_inc(fh_ready, 1)
                with act.Fori(0, 2) as i:
                    for q in range(4):
                        act.wait_ge(bank_free[q], q0 + i + (TILE_D // 4 + 2))
                        square(l * 16 + i * 4 + (16 + q), i * 4 + q, q % 2)

            norm(2 * L)
            for b in range(NB):
                act.wait_ge(out_turned, 2 * b + 2)
                act.wait_ge(out_ready, 2 * b + 1)
                copy(y_tok[:, b, 512:1024], bank[2 * b + 1][:]).then_inc(out_ready, 1)

        @block.vector
        def _(dve):
            def tt(o, a, b_, op):
                return dve.tensor_tensor(o, a, b_, op)

            def chunk(buf, c):
                return buf[:, ds(c, 1), :].rearrange("p a t -> p (a t)")

            dve.memset(ones[:], 1.0).then_inc(split_done, SLOTS)
            dve.memset(epsc[:], EPS).then_inc(units_begun, SLOTS - 1)
            for b in range(4):
                dve.memset(rms[:, :, b:b + 1], 0.0).then_inc(bank_free[b], 1)
            dve.memset(ssq[:], 0.0).then_inc(pv_taken, 1)
            for c in range(DC):
                dve.wait_ge(x_turned, c + 1)
                dve.tensor_copy(h[:, c, :], bank[c][:]).then_inc(h_loaded, 1)

            def add_square(i8, par):
                dve.wait_ge(sq_ready, i8 + 1)
                tt(ssq[:], ssq[:], sq[:, par, :], ALU.add).then_inc(ssq_added, 1)
                dve.drain()

            for c in range(DC):
                add_square(c, c % 2)

            def norm(i, gain0, out_chunk, u0):
                dve.wait_ge(std_ready, i + 1)
                dve.reciprocal(rms[:, 1, :], rms[:, 0, :])
                dve.memset(ssq[:], 0.0)
                dve.drain()
                dve.tensor_copy(rb[:], rms[:, 1, :].unsqueeze(2).broadcast_to([P, NB, P])).then_inc(rb_ready, 1)
                dve.wait_ge(rstd_ready, i + 1)

                def scale(c):
                    o = ut[:, c % 2, :] if out_chunk is None else out_chunk(c)
                    ins = dve.scalar_tensor_tensor(o, h[:, c, :], prm[:, ds(gain0 + c, 1)], bank[5][:], ALU.mult, ALU.mult)
                    ins.then_inc(ut_ready if out_chunk is None else final_ready, 1)

                def low(c):
                    dve.wait_ge(uh_ready, u0 + (c + 1))
                    tt(ul[:, c, :], ut[:, c % 2, :], uh[:, c, :].bitcast(F32), ALU.subtract).then_inc(u_ready, 1)

                scale(0)
                for c in range(1, DC):
                    scale(c)
                    if out_chunk is None:
                        low(c - 1)
                        dve.drain()
                if out_chunk is None:
                    low(DC - 1)

            def rope(b):
                xa = tcols(b, AQ, 640).rearrange("p (h x) -> p h x", x=DH)[:, :, 0:ROT].rearrange("p h (t x) -> p h t x", t=2)
                xr = tcols(b, RQ, 512).rearrange("p (h t x) -> p h t x", t=2, x=32)
                br = blk[:, 768:1280].rearrange("p (h t x) -> p h t x", t=2, x=32)
                ta = tmp[:, 0:160].rearrange("p (h t x) -> p h t x", t=2, x=8)
                tr = tmp[:, 160:672].rearrange("p (h t x) -> p h t x", t=2, x=32)

                def table(c0, half, heads):
                    return cst[:, ds(b * half + c0, half)].unsqueeze(1).unsqueeze(1).broadcast_to([P, heads, 2, half])

                tt(ta, xa, table(C_SINA, 8, 10), ALU.mult)
                tt(tr, xr, table(C_SINR, 32, 8), ALU.mult)
                tt(xa, xa, table(C_COSA, 8, 10), ALU.mult)
                tt(br, xr, table(C_COSR, 32, 8), ALU.mult)
                dve.drain()
                tt(xa[:, :, 0, :], xa[:, :, 0, :], ta[:, :, 1, :], ALU.subtract)
                tt(xa[:, :, 1, :], xa[:, :, 1, :], ta[:, :, 0, :], ALU.add)
                tt(br[:, :, 0, :], br[:, :, 0, :], tr[:, :, 1, :], ALU.subtract)
                tt(br[:, :, 1, :], br[:, :, 1, :], tr[:, :, 0, :], ALU.add)
                dve.drain()
                dve.tensor_copy(blk[:, 0:512], tcols(b, AQ, 512))
                dve.tensor_copy(blk[:, 1536:2048], tcols(b, RV, 512))
                dve.tensor_copy(blk[:, 512:768].rearrange("p (g r x) -> p g r x", g=2, r=2),
                                tcols(b, AK, 128).rearrange("p (g x) -> p g x", g=2).unsqueeze(2).broadcast_to([P, 2, 2, DH]))
                tt(blk[:, 1280:1536].rearrange("p (h x) -> p h x", h=RH), blk[:, 1024:1280].rearrange("p (h x) -> p h x", h=RH),
                   cst[:, C_ZETA:C_ZETA + RH].unsqueeze(2).broadcast_to([P, RH, RDK]), ALU.mult).then_inc(rope_done, 1)

            def block_step(l, b, q0, more):
                B = l * NB + b
                t = l * TILES + b * 4 + TILE_B
                dve.wait_ge(taken_qk, B * 3 + 2)
                tt(qx[:], rT[:, 0:256].rearrange("p (a t) -> p a t", a=2),
                   cst[:, C_XI:C_XI + 256].rearrange("p (a t) -> p a t", a=2), ALU.mult).then_inc(qx_ready, 1)
                mask = cst[:, ds(b * 256 + C_MASK, 256)].unsqueeze(1).broadcast_to([P, 2, 256])
                for i in range(4):
                    dve.wait_ge(scores_full, B * 4 + (i + 1))
                    dve.scalar_tensor_tensor(S_sb[:, 2 * i:2 * i + 2, :], bank[4 + i][:].rearrange("p (a t) -> p a t", a=2),
                                             DH ** -0.5, mask, ALU.mult, ALU.add).then_inc(scores_taken, 1)
                dve.drain()
                dve.reduce_max(mx[:], S_sb[:], AXIS_X)
                dve.drain()
                sink = sinks[:, ds(l * HQ, HQ)].rearrange("p (a r) -> p r a", r=2)
                as2 = lambda v: v[:].rearrange("p (r a) -> p r a", r=2)
                tt(as2(mx), as2(mx), sink, ALU.max)
                dve.drain()
                dve.tensor_scalar(negm[:], mx[:], -1.0, None, ALU.mult)
                tt(as2(sinkm), sink, as2(mx), ALU.subtract).then_inc(max_ready, 1)
                for par in range(2):
                    dve.wait_ge(ret_full, B * 3 + (par + 1))
                    at = C_DMASK + 256 * par
                    tt(att[:, par, :, :], bank[7 - par][:, 0:256].rearrange("p (a t) -> p a t", a=2),
                       cst[:, at:at + 256].rearrange("p (a t) -> p a t", a=2), ALU.mult).then_inc(att_ready, 1)
                full(dve, t + 1)
                dve.wait_ge(bank_free[0], q0 + b + (TILE_B // 4 + 2))
                tt(ub[:, 2:S + 2], bank[1][:], ccs[:], ALU.mult).then_inc(bank_free[1], 1)
                dve.drain()
                w = lambda i: prm[:, ds(l * 12 + b + (R_CONV + 4 * i), 1)]
                dve.tensor_scalar(ccs[:], ub[:, 0:S], w(0), None, ALU.mult)
                dve.drain()
                for i in (1, 2):
                    dve.scalar_tensor_tensor(ccs[:], ub[:, i:S + i], w(i), ccs[:], ALU.mult, ALU.add)
                    dve.drain()
                dve.wait_ge(ret_full, B * 3 + 3)
                dve.wait_ge(y_full, B + 1)
                for hd in range(RH):
                    par, j = hd % 2, hd // 2
                    half = slice(64 * par, 64 * par + 64)
                    ins = dve.scalar_tensor_tensor(state[half, hd, :], state[half, hd, :], cst[half, C_DECAY + j:C_DECAY + j + 1],
                                                   bank[5][half, j * P:j * P + P], ALU.mult, ALU.add)
                ins.then_inc(state_ready, 1)
                for n, bk in ((2, 6), (4, 4)):
                    dve.wait_ge(probs_turned, B * 4 + n)
                    dve.tensor_copy(PT[:, n - 1, :, :], bank[bk][:].rearrange("p (a t) -> p a t", a=4)).then_inc(probs_v, 1)
                if more:
                    rope(b + 1)
                dve.wait_ge(bank_free[2], q0 + b + (TILE_B // 4 + 2))
                tt(ccs[:], ccs[:], cbs[:], ALU.mult).then_inc(conv_ready, 1)
                dve.wait_ge(exp_done, B * 9 + 9)
                tt(rden[:], sums[:], sinkm[:], ALU.add)
                dve.drain()
                dve.reciprocal(rden[:], rden[:])
                dve.wait_ge(hi_ready, l * 12 + b + 1)
                tt(chunk(bl, b), ccs[:], chunk(bh, b).bitcast(F32), ALU.subtract).then_inc(branch_ready, 1)
                dve.drain()
                dve.wait_ge(pv_full, B + 1)
                dve.tensor_copy(vprev[:], tcols(b, AV, P))
                tt(tcols(b, AQ, 512).rearrange("p (a r x) -> p r a x", r=2, x=DH),
                   bank[7][:].rearrange("p (a r x) -> p r a x", r=2, x=DH),
                   as2(rden).unsqueeze(3).broadcast_to([P, 2, 4, DH]), ALU.mult).then_inc(pv_taken, 1)

            with dve.Fori(0, L) as l:
                t0 = l * TILES
                q0 = l * (TILES // 4)
                norm(l * 2, l * DC + R_MIX, None, l * 24)
                dve.memset(kwin[:], 0.0)
                dve.memset(vprev[:], 0.0)
                dve.memset(ub[:, 0:2], 0.0)
                dve.memset(state[:], 0.0).then_inc(state_ready, 1)
                dve.wait_ge(bank_free[3], q0 + (TILE_B // 4 + 1))
                dve.wait_ge(bank_free[2], q0 + (TILE_B // 4 + 1))
                dve.wait_ge(bank_free[1], q0 + (TILE_B // 4 + 1))
                dve.wait_ge(bank_free[0], q0 + (TILE_B // 4 + 1))
                rope(0)
                with dve.Fori(0, NB - 1) as b:
                    block_step(l, b, q0, True)
                block_step(l, NB - 1, q0, False)

                dve.wait_ge(gate_ready, l + 1)
                for q in range(4):
                    full(dve, t0 + (TILE_C + q))
                    tt(m[:, q, :], sg[:, q, :], bank[q][:], ALU.mult).then_inc(bank_free[q], 1)
                rt = tok[:, :, RQ:RQ + 512]
                gt = tok[:, :, RG:TOKW]
                dve.wait_ge(ret_std, l + 1)
                dve.reciprocal(ssqR[:], rstdR[:])
                dve.wait_ge(y_taken, l * NB + NB)
                tt(rt, rt, gt, ALU.mult).then_inc(ret_g, 1)
                dve.drain()
                dve.wait_ge(ret_sig, l + 1)
                for b in range(NB):
                    for hd in range(RH):
                        c = slice(hd * P, hd * P + P)
                        ins = dve.scalar_tensor_tensor(rt[:, b, c], rt[:, b, c], ssqR[:, b * RH + hd:b * RH + hd + 1],
                                                       gt[:, b, c], ALU.mult, ALU.mult)
                ins.then_inc(ret_gated, 1)
                for q in range(4):
                    dve.wait_ge(bank_free[q], q0 + (TILE_C // 4 + 3))
                    full(dve, t0 + (TILE_C + 8 + q))
                    tt(m[:, 4 + q, :], sg[:, q, :], bank[q][:], ALU.mult).then_inc(bank_free[q], 1)
                with dve.Fori(0, 2) as i:
                    for c in range(4):
                        dve.wait_ge(hi_ready, l * 12 + i * 4 + (5 + c))
                        src = tokf[:, ds(i * 512 + (c * TOKW + RV), 512)]
                        tt(bl[:, c, :], src, bh[:, c, :].bitcast(F32), ALU.subtract).then_inc(branch_ready, 1)
                    for g in range(2):
                        for q in range(4):
                            dve.wait_ge(bank_free[q], q0 + i * 4 + (TILE_M // 4 + 2 * g + 2))
                            full(dve, t0 + i * 16 + (TILE_M + 8 * g + 4 + q))
                            tt(prod[:], sg[:, q, :], bank[q][:], ALU.mult).then_inc(bank_free[q], 1)
                            dve.drain()
                            tt(m[:, 4 * g + q, :], m[:, 4 * g + q, :], prod[:], ALU.add).then_inc(m_ready, 1)
                            dve.drain()
                for c in range(DC):
                    dve.wait_ge(uh_ready, l * 24 + (8 + c + 1))
                    tt(ul[:, c, :], m[:, c, :], uh[:, c, :].bitcast(F32), ALU.subtract).then_inc(u_ready, 1)

                def into_h(i8, t, c):
                    for q in range(4):
                        full(dve, t + q)
                        tt(chunk(h, c + q), chunk(h, c + q), bank[q][:], ALU.add).then_inc(bank_free[q], 1)
                        if q:
                            add_square(i8 + (q - 1), (q - 1) % 2)
                    add_square(i8 + 3, 1)

                dve.drain()
                dve.memset(ssq[:], 0.0)
                dve.drain()
                with dve.Fori(0, 2) as i:
                    into_h(l * 16 + i * 4 + 8, t0 + i * 4 + TILE_O, i * 4)
                norm(l * 2 + 1, l * DC + R_FFN, None, l * 24 + 16)
                with dve.Fori(0, FC // 2) as i:
                    t = t0 + i * 4 + TILE_G
                    for q in range(2):
                        dve.wait_ge(sig_ready, l * FC + i * 2 + (q + 1))
                        tt(gp[:], sgt[:], bank[2 * q][:], ALU.mult).then_inc(bank_free[2 * q], 1)
                        dve.drain()
                        full(dve, t + (2 * q + 1))
                        tt(ft[:], gp[:], bank[2 * q + 1][:], ALU.mult).then_inc(bank_free[2 * q + 1], 1)
                        dve.wait_ge(fh_ready, l * FC + i * 2 + (q + 1))
                        tt(chunk(fl, i * 2 + q), ft[:], chunk(fh, i * 2 + q).bitcast(F32), ALU.subtract).then_inc(f_ready, 1)
                        dve.drain()
                with dve.Fori(0, 2) as i:
                    into_h(l * 16 + i * 4 + 16, t0 + i * 4 + TILE_D, i * 4)

            norm(2 * L, R_FIN, lambda c: y_fm[:, c, :], None)
            for b in range(NB):
                if b:
                    dve.wait_ge(out_ready, 2 * b)
                dve.wait_ge(out_turned, 2 * b + 1)
                dve.tensor_copy(y_tok[:, b, 0:512], bank[2 * b][:]).then_inc(out_ready, 1)


_INS = ["x", "norm_mix", "w_in", "attn_sinks", "conv_w", "w_branch", "b_gate", "w_out",
        "norm_ffn", "w_ffn_gate", "w_ffn_up", "w_ffn_down", "norm_final"]


def kernel(**inputs):
    import concourse.bacc as bacc
    from concourse.bass_utils import run_bass_kernel_spmd

    arrays = {name: np.ascontiguousarray(inputs[name]) for name in _INS}
    arrays["consts"] = shape_constants(arrays["x"].shape[1])
    nc = bacc.Bacc("TRN2", target_bir_lowering=False, num_devices=1, dynamic_dma_scratch_size=1024)
    args = [nc.dram_tensor(n, a.shape, mybir.dt.from_np(a.dtype), kind="ExternalInput").ap() for n, a in arrays.items()]
    out = nc.dram_tensor("out", arrays["x"].shape, F32, kind="ExternalOutput").ap()
    trunk(nc, *args, out)
    return run_bass_kernel_spmd(nc, [arrays], core_ids=[0]).results[0]["out"]
```

```python
from contextlib import ExitStack

import numpy as np
import concourse.bass as bass
from concourse import mybir
from concourse.bass import ds

F32 = mybir.dt.float32
F32R = mybir.dt.float32r
ALU = mybir.AluOpType
ACT = mybir.ActivationFunctionType
AXIS_X = mybir.AxisListType.X

P = 128
EPS = 1e-6
ROPE_THETA, RET_ROPE_THETA = 500000.0, 10000.0

HQ, HKV, DH, ROT = 8, 2, 64, 16
RH, RDK, RDV = 4, 64, 128
AQ, AK, AV, RQ, RK, RV, RG, TOKW = 0, 512, 640, 768, 1024, 1280, 1792, 2304
CB, CC, CX, GATES = 2304, 2816, 3328, 3840

C_ID = 0
C_MASK = C_ID + P
C_DMASK = C_MASK + 4 * 256
C_XI = C_DMASK + 4 * P
C_COSA = C_XI + 2 * P
C_SINA = C_COSA + 32
C_COSR = C_SINA + 32
C_SINR = C_COSR + 128
C_ZETA = C_SINR + 128
C_DECAY = C_ZETA + RH
C_ALL = C_DECAY + 2


def shape_constants(S):
    out = np.zeros((P, C_ALL), np.float32)
    NB = S // P
    out[:, C_ID:C_ID + P] = np.eye(P)
    qi, kj = np.arange(P)[:, None], np.arange(2 * P)[None]
    diff = P + qi - kj
    for b in range(4):
        keep = (diff >= 0) & (diff < P) & ((b - 1) * P + kj >= 0)
        out[:, C_MASK + 256 * b:C_MASK + 256 * (b + 1)] = np.where(keep, 0.0, -3.0e38)
    idx = np.arange(P, dtype=np.float64)
    gamma = 1.0 - np.exp2(-(5.0 + np.arange(RH)))
    for h in range(RH):
        par, j = h % 2, h // 2
        rel = idx[None] - idx[:, None]
        at = C_DMASK + h * P
        out[:, at:at + P] = np.where(rel >= 0, gamma[h] ** np.maximum(rel, 0), 0.0) * RDK ** -0.5
        rows = slice(64 * par, 64 * par + 64)
        out[rows, C_XI + j * P:C_XI + (j + 1) * P] = gamma[h] ** (idx + 1)
        out[:, C_ZETA + h] = gamma[h] ** (P - 1 - idx) * RDK ** -0.5
        out[rows, C_DECAY + j] = gamma[h] ** P
    for half, theta, c_cos, c_sin in ((ROT // 2, ROPE_THETA, C_COSA, C_SINA),
                                      (RDK // 2, RET_ROPE_THETA, C_COSR, C_SINR)):
        inv = np.float32(theta) ** (-np.arange(half, dtype=np.float32) / np.float32(half))
        ang = (np.arange(S, dtype=np.float32)[:, None] * inv[None]).astype(np.float64)
        for b in range(NB):
            out[:, c_cos + b * half:c_cos + (b + 1) * half] = np.cos(ang[b * P:(b + 1) * P])
            out[:, c_sin + b * half:c_sin + (b + 1) * half] = np.sin(ang[b * P:(b + 1) * P])
    return out


def trunk(nc, x, norm_mix, w_in, attn_sinks, conv_w, w_branch, b_gate, w_out,
          norm_ffn, w_ffn_gate, w_ffn_up, w_ffn_down, norm_final, consts, out):
    _, S, D = x.shape
    L = w_in.shape[0]
    FF = w_ffn_gate.shape[2]
    NB, DC, FC = S // P, D // P, FF // P
    assert (NB, DC, FC, L) == (4, 8, 22, 2) and w_in.shape[2] == GATES + 3 * D

    SLOTS = 4
    LEAD = 16
    UNIT_A, UNIT_B, UNIT_C, UNIT_M, UNIT_O, UNIT_G, UNIT_D, UNITS = 0, 18, 34, 42, 66, 74, 118, 140
    TILE_A, TILE_B, TILE_C, TILE_M, TILE_O, TILE_G, TILE_D, TILES = 0, 20, 36, 48, 80, 88, 132, 140
    assert UNITS % SLOTS == 0 and TILES % 4 == 0
    HEAD = [0, 2, 4, 6, 1, 3, 5, 7]
    R_MIX = 0
    R_FFN = R_MIX + (L + 1) * DC
    R_BG = R_FFN + L * DC
    R_CONV = R_BG + 3 * L * DC
    R_ALL = R_CONV + L * 12

    with ExitStack() as ctx:
        def sb(name, shape, dt=F32, at=ctx):
            return at.enter_context(nc.sbuf_tensor(name, shape, dt))

        def sem(name):
            return ctx.enter_context(nc.semaphore(name))

        h = sb("h", [P, DC, S])
        uh = sb("uh", [P, DC, S], F32R)
        ul = sb("ul", [P, DC, S], F32R)
        raw = sb("raw", [P, SLOTS, 1024])
        wh = sb("wh", [P, SLOTS, 1024], F32R)
        wl = sb("wl", [P, SLOTS, 1024], F32R)
        cst = sb("cst", [P, C_ALL])
        prm = sb("prm", [P, R_ALL])
        sinks = sb("sinks", [P, L * HQ])
        ones = sb("ones", [P, LEAD])
        epsc = sb("epsc", [P, 1])
        ident_r = sb("ident_r", [P, P], F32R)
        rms = sb("rms", [P, NB])
        rs = sb("rs", [P, NB])
        rsF = sb("rsF", [P, S])
        rs2F = sb("rs2F", [P, S])
        with ExitStack() as one:
            tok = sb("tok", [P, NB, TOKW], at=one)
            bh = sb("bh", [P, 4, S], F32R, at=one)
            bl = sb("bl", [P, 4, S], F32R, at=one)
            sg = sb("sg", [P, 4, S], at=one)
            cbs = sb("cbs", [P, S], at=one)
            ccs = sb("ccs", [P, S], at=one)
            ub = sb("ub", [P, S + 2], at=one)
            blk = sb("blk", [P, 2048], at=one)
            tmp = sb("tmp", [P, 10 * ROT + 8 * RDK], at=one)
            qs = sb("qs", [P, 2, 4, P], F32R, at=one)
            qpad = sb("qpad", [P, 2, 2, P], at=one)
            rkT = sb("rkT", [P, 2, P], at=one)
            kwin = sb("kwin", [P, 2, 2, 256], F32R, at=one)
            att = sb("att", [P, RH, P], at=one)
        with ExitStack() as two:
            fh = sb("fh", [P, FC, S], F32R, at=two)
            fl = sb("fl", [P, FC, S], F32R, at=two)
        with ExitStack() as three:
            mh = sb("mh", [P, DC, S], F32R, at=three)
            ml = sb("ml", [P, DC, S], F32R, at=three)
        size_one = 4 * (NB * TOKW + 3 * 4 * S + 2 * S + S + 2 + 2048 + 10 * ROT + 8 * RDK + 3072 + 256)
        assert 2 * DC * S <= NB * TOKW
        region1 = sb("region1", [P, max(size_one, 8 * FC * S) // 4 + 8])
        with ExitStack() as one:
            S_sb = sb("S_sb", [P, 8, 256], at=one)
            PT = sb("PT", [P, 4, 4, P], at=one)
        with ExitStack() as two:
            m = sb("m", [P, DC, S], at=two)
        with ExitStack() as three:
            rb = sb("rb", [P, NB, P], at=three)
            sq = sb("sq", [P, 2, S], at=three)
            ssq = sb("ssq", [P, S], at=three)
            sgt = sb("sgt", [P, S], at=three)
            gp = sb("gp", [P, S], at=three)
            ft = sb("ft", [P, S], at=three)
        region2 = sb("region2", [P, DC * S])
        vprev = sb("vprev", [P, P])
        qx = sb("qx", [P, 2, P])
        state = sb("state", [P, RH, P])
        prod = sb("prod", [P, S])
        mx, negm, sinkm, sums, rden = (sb(n, [P, 8]) for n in ("mx", "negm", "sinkm", "sums", "rden"))
        ssqR = sb("ssqR", [P, NB * RH])
        rstdR = sb("rstdR", [P, NB * RH])

        bank = [ctx.enter_context(nc.psum_tensor(f"bank{i}", [P, 512], F32)) for i in range(8)]

        tokf = tok[:].rearrange("p b c -> p (b c)")
        ident = cst[:, C_ID:C_ID + P]

        def tcols(b, c, n):
            return tokf[:, ds(b * TOKW + c, n)]

        x_tok = tokf[:, 0:NB * D].rearrange("p (b c) -> p b c", b=NB)
        y_tok = x_tok
        yfm = tok[:, :, RV:RV + 1024].rearrange("p c (w t) -> p w c t", w=2)

        x_in = [sem(f"x_in{b}") for b in range(NB)]
        params_in = sem("params_in")
        ident_in = sem("ident_in")
        consts_in = sem("consts_in")
        raw_full = [sem(f"raw_full{s}") for s in range(SLOTS)]
        split_done = sem("split_done")
        units_begun = sem("units_begun")
        tile_full = sem("tile_full")
        bank_free = [sem(f"bank_free{b}") for b in range(4)]
        x_turned = sem("x_turned")
        h_loaded = sem("h_loaded")
        identr_ready = sem("identr_ready")
        params_turned = sem("params_turned")
        params_ready = sem("params_ready")
        uh_ready = sem("uh_ready")
        u_ready = sem("u_ready")
        sq_ready = sem("sq_ready")
        ssq_added = sem("ssq_added")
        ms_ready = sem("ms_ready")
        std_ready = sem("std_ready")
        rs_ready = sem("rs_ready")
        rb_ready = sem("rb_ready")
        rs_turned = sem("rs_turned")
        rsF_ready = sem("rsF_ready")
        rope_done = sem("rope_done")
        turned_qk = sem("turned_qk")
        taken_qk = sem("taken_qk")
        qx_ready = sem("qx_ready")
        scores_full = sem("scores_full")
        scores_taken = sem("scores_taken")
        max_ready = sem("max_ready")
        exp_done = sem("exp_done")
        ret_full = sem("ret_full")
        att_ready = sem("att_ready")
        y_full = sem("y_full")
        y_taken = sem("y_taken")
        state_ready = sem("state_ready")
        probs_turned = sem("probs_turned")
        probs_a = sem("probs_a")
        probs_v = sem("probs_v")
        pv_full = sem("pv_full")
        pv_taken = sem("pv_taken")
        conv_ready = sem("conv_ready")
        hi_ready = sem("hi_ready")
        branch_ready = sem("branch_ready")
        ret_std = sem("ret_std")
        ret_g = sem("ret_g")
        ret_sig = sem("ret_sig")
        ret_gated = sem("ret_gated")
        branch_turned = sem("branch_turned")
        branch_taken = sem("branch_taken")
        gate_ready = sem("gate_ready")
        m_ready = sem("m_ready")
        mh_ready = sem("mh_ready")
        ml_ready = sem("ml_ready")
        f_raw = sem("f_raw")
        sig_ready = sem("sig_ready")
        fh_ready = sem("fh_ready")
        f_ready = sem("f_ready")
        out_turned = sem("out_turned")
        out_ready = [sem("out_ready_v"), sem("out_ready_a")]
        out_sent = sem("out_sent")

        LEAVES = [(0, 0), (0, 1), (0, 2), (0, 3), (1, 1), (1, 2), (1, 3), (1, 0)]

        def full(eng, t):
            eng.wait_ge(tile_full, t + 1)

        block = ctx.enter_context(nc.Block())

        @block.sync
        def _(sp):
            xb = x.rearrange("a (b p) d -> p (a b) d", p=P)
            sp.dma_start(cst[:, 0:P], consts[:, 0:P]).then_inc(ident_in, 16)
            for b in range(NB - 1):
                sp.dma_start(x_tok[:, b, :], xb[:, b, :]).then_inc(x_in[b], 16)
            src = conv_w.rearrange("l i (c p) -> (l i c) p", p=P)
            sp.dma_start(blk[R_CONV:R_CONV + src.shape[0], 0:P], src).then_inc(params_in, 16)

            def load(n, slot, src, k):
                sp.wait_ge(split_done, n + 1)
                sp.dma_start(raw[:, slot, :].rearrange("p (k n) -> p k n", k=k), src).then_inc(raw_full[slot], 16)

            def rows(w, lead, r0, nk, c0, nc_):
                return w[ds(lead, 1), ds(r0, nk * P), ds(c0, nc_)].rearrange("a (k p) n -> p (a k) n", p=P)

            wb = w_branch.rearrange("l i c d -> (l i) c d")

            with sp.Fori(0, L) as l:
                n0 = l * UNITS
                with sp.Fori(0, 4) as g:
                    for j in range(4):
                        load(n0 + g * 4 + j, j, rows(w_in, l, 2 * P * j, 2, g * 512, 512), 2)
                for j in range(2):
                    load(n0 + 16 + j, j, rows(w_in, l, 4 * P * j, 4, 2048, 256), 4)
                with sp.Fori(0, 4) as j:
                    for q, c0 in enumerate((CC, CX, CB, GATES + 2 * D)):
                        load(n0 + j * 4 + (UNIT_B + q), (UNIT_B + q) % SLOTS, rows(w_in, l, 0, 8, j * P + c0, P), 8)

                def gate_units(n, i, g, off):
                    for q in range(4):
                        load(n + q, (off + q) % SLOTS, rows(w_in, l, 0, 8, i * D + (GATES + (4 * g + q) * P), P), 8)

                def branch_units(n, i, g, off):
                    for q in range(2):
                        load(n + q, (off + q) % SLOTS, rows(wb, l * 3 + i, 0, 4, 512 * g + 256 * q, 256), 4)

                branch_units(n0 + UNIT_C, 2, 0, UNIT_C)
                gate_units(n0 + (UNIT_C + 2), 2, 1, UNIT_C + 2)
                branch_units(n0 + (UNIT_C + 6), 2, 1, UNIT_C + 6)
                with sp.Fori(0, 2) as i:
                    for g in range(2):
                        gate_units(n0 + i * 12 + (UNIT_M + 6 * g), i, g, UNIT_M + 6 * g)
                        branch_units(n0 + i * 12 + (UNIT_M + 6 * g + 4), i, g, UNIT_M + 6 * g + 4)
                with sp.Fori(0, 2) as i:
                    for q in range(4):
                        load(n0 + i * 4 + (UNIT_O + q), (UNIT_O + q) % SLOTS, rows(w_out, l, 0, 8, i * 512 + q * P, P), 8)
                with sp.Fori(0, FC // 2) as i:
                    for q in range(4):
                        w = w_ffn_up if q % 2 else w_ffn_gate
                        load(n0 + i * 4 + (UNIT_G + q), (UNIT_G + q) % SLOTS, rows(w, l, 0, 8, i * 256 + (q // 2) * P, P), 8)
                for half in range(2):
                    def down(j, n, off):
                        load(n0 + n, off % SLOTS, rows(w_ffn_down, l, j * 256, 2, 512 * half, 512), 2)
                    u0 = UNIT_D + 11 * half
                    down(0, u0, u0)
                    with sp.Fori(0, 2) as i:
                        for q in range(4):
                            down(i * 4 + (1 + q), i * 4 + (u0 + 1 + q), u0 + 1 + q)
                    down(9, u0 + 9, u0 + 9)
                    down(10, u0 + 10, u0 + 10)

            for n, (half, b) in enumerate(LEAVES):
                sp.wait_ge(out_ready[n % 2], n // 2 + 1)
                cols = slice(512 * half, 512 * half + 512)
                sp.dma_start(out.rearrange("a (b p) d -> p (a b) d", p=P)[:, b, cols], y_tok[:, b, cols]).then_inc(out_sent, 16)
            sp.wait_ge(out_sent, 16 * 2 * NB)

        @block.gpsimd
        def _(pool):
            with pool.Fori(0, L * UNITS // SLOTS) as q:
                for s in range(SLOTS):
                    pool.wait_ge(raw_full[s], q * 16 + 16)
                    pool.wait_ge(units_begun, q * 4 + (s + 1))
                    pool.tensor_tensor(wh[:, s, 0:LEAD], raw[:, s, 0:LEAD], ones[:], ALU.mult)
                    pool.tensor_scalar(wh[:, s, LEAD:], raw[:, s, LEAD:], 1.0, 0.0, ALU.mult, ALU.add)
                    pool.drain()
                    for half in (slice(0, 512), slice(512, 1024)):
                        ins = pool.tensor_tensor(wl[:, s, half], raw[:, s, half], wh[:, s, half].bitcast(F32), ALU.subtract)
                    ins.then_inc(split_done, 1)

        @block.tensor
        def _(pe):
            def begin(n):
                pe.wait_ge(split_done, n + 1 + SLOTS)

            def may_write(t4, b):
                pe.wait_ge(bank_free[b], t4 + 1)

            def turn(dst, src):
                return pe.transpose(dst, src, ident)

            def feature_unit(n, slot, t4, b, xh, xl, nk, width=P, c0=0, first=True, waits=None, midway=None):
                if first:
                    begin(n)
                may_write(t4, b)
                a = wh[:, slot, :].rearrange("p (k n) -> p k n", k=nk)
                r = wl[:, slot, :].rearrange("p (k n) -> p k n", k=nk)
                cols = slice(c0, c0 + P)
                for k in range(nk):
                    if midway is not None and k == nk // 2:
                        midway()
                    if waits is not None:
                        pe.wait_ge(*waits(k))
                    mm = pe.matmul(bank[b][:], a[:, k, cols], xh[:, k, :], start=k == 0, stop=False)
                    if first and k == 0:
                        mm.then_inc(units_begun, 1)
                    pe.matmul(bank[b][:], a[:, k, cols], xl[:, k, :], start=False, stop=False)
                    mm = pe.matmul(bank[b][:], r[:, k, cols], xh[:, k, :], start=False, stop=k == nk - 1)
                mm.then_inc(tile_full, 1)

            def token_product(b, k, slot, kk, width, nk, start, stop):
                a = wh[:, slot, :].rearrange("p (k n) -> p k n", k=nk)[:, kk, :]
                r = wl[:, slot, :].rearrange("p (k n) -> p k n", k=nk)[:, kk, :]
                t = slice(b * P, b * P + P)
                o = bank[b][:, 0:width]
                first = pe.matmul(o, uh[:, k, t], a, start=start, stop=False)
                pe.matmul(o, uh[:, k, t], r, start=False, stop=False)
                return first, pe.matmul(o, ul[:, k, t], a, start=False, stop=stop)

            def token_group(n, t4, units, nk, width, u0=None, before={}):
                for j in range(units):
                    begin(n + j)
                    last = j == units - 1
                    order = [(kk, b) for kk in range(nk) for b in range(NB)]
                    if last:
                        order = [(kk, b) for b in range(NB) for kk in range(nk)]
                    for at, (kk, b) in enumerate(order):
                        k = nk * j + kk
                        if (j, at) in before:
                            before[j, at]()
                        if u0 is not None:
                            pe.wait_ge(u_ready, u0 + k + 1)
                        if k == 0:
                            may_write(t4, b)
                        first, mm = token_product(b, k, j, kk, width, nk, k == 0, k == DC - 1)
                        if at == 0:
                            first.then_inc(units_begun, 1)
                        if k == DC - 1:
                            mm.then_inc(tile_full, 1)

            def sum_squares(i, bk=4, c0=0):
                pe.wait_ge(ssq_added, i * 8 + (8 + 2))
                for b in range(NB):
                    mm = pe.matmul(bank[bk][:, c0 + b:c0 + b + 1], ssq[:, b * P:b * P + P], ones[:, 0:1], start=True, stop=True)
                mm.then_inc(ms_ready, 1)

            def spread(i):
                pe.wait_ge(rb_ready, i + 1)
                for b in range(NB):
                    mm = turn(bank[5][:, b * P:b * P + P], rb[:, b, :])
                mm.then_inc(rs_turned, 1)

            def block_turn(B):
                pe.wait_ge(rope_done, B + 1)
                for c in range(4):
                    mm = turn(bank[4][:, c * P:c * P + P], blk[:, c * P:c * P + P])
                mm.then_inc(turned_qk, 1)
                for c in range(4):
                    mm = turn(bank[5][:, c * P:c * P + P], blk[:, 768 + c * P:896 + c * P])
                mm.then_inc(turned_qk, 1)
                for c in range(2):
                    mm = turn(bank[6][:, c * P:c * P + P], blk[:, 512 + c * P:640 + c * P])
                mm.then_inc(turned_qk, 1)

            def block_scores(B):
                pe.wait_ge(qx_ready, B + 1)
                pe.wait_ge(pv_taken, B + 1)
                for i in range(2):
                    for par in range(2):
                        for s in range(2):
                            pair = 2 * i + s
                            for part in range(2):
                                mm = pe.matmul(bank[4 + 2 * par + i][:, 256 * s:256 * s + 256], qs[:, par, pair, :],
                                               kwin[:, part, pair // 2, :], start=part == 0, stop=part == 1)
                        mm.then_inc(scores_full, 1)

            def block_ret(B):
                pe.wait_ge(scores_taken, B * 4 + 4)
                for j in range(2):
                    mm = pe.matmul(bank[7][:, 256 * j:256 * j + 256], rkT[:, j, :], qpad[:, j, :, :], start=True, stop=True)
                mm.then_inc(ret_full, 1)
                for j in range(2):
                    mm = pe.matmul(bank[6][:, 256 * j:256 * j + 256], blk[:, 1280 + P * j:1408 + P * j],
                                   blk[:, 1536 + 256 * j:1792 + 256 * j], start=True, stop=True)
                mm.then_inc(ret_full, 1)

            def block_ret_out(l, b, B, first):
                if not first:
                    pe.wait_ge(state_ready, l * (NB + 1) + b + 1)
                    for j in range(2):
                        pe.matmul(bank[4][:, 256 * j:256 * j + 256], qx[:, j, :], state[:, 2 * j:2 * j + 2, :],
                                  start=j == 0, stop=False, skip_group_check=True)
                pe.wait_ge(att_ready, B + 1)
                for hd in range(RH):
                    mm = pe.matmul(bank[4][:, hd * P:hd * P + P], att[:, hd, :], blk[:, 1536 + hd * P:1664 + hd * P],
                                   start=first and hd == 0, stop=hd == RH - 1, skip_group_check=True)
                mm.then_inc(y_full, 1)

            def block_probs(l, b, B, first):
                for s in range(8):
                    pe.wait_ge(exp_done, B * 9 + (s + 1))
                    if s == 4:
                        pe.wait_ge(state_ready, l * (NB + 1) + b + 2)
                        pe.wait_ge(y_taken, B + 1)
                    for c in range(first, 2):
                        bk = (7, 5)[c] if s < 4 else (6, 4)[c]
                        mm = turn(bank[bk][:, (s % 4) * P:(s % 4) * P + P], S_sb[:, s, c * P:c * P + P])
                        if s % 4 == 3:
                            mm.then_inc(probs_turned, 1 + first)

            def block_pv(b, B, first):
                pe.wait_ge(probs_a, B * 2 + 2)
                pe.wait_ge(probs_v, B * 2 + 2)
                for s in range(8):
                    hd = HEAD[s]
                    kv = hd // 4
                    o = bank[7][:, hd * DH:hd * DH + DH]
                    if not first:
                        pe.matmul(o, PT[:, 2 * (s // 4), s % 4, :], vprev[:, kv * DH:kv * DH + DH], start=True, stop=False)
                    mm = pe.matmul(o, PT[:, 2 * (s // 4) + 1, s % 4, :], tcols(b, AV + kv * DH, DH), start=first, stop=True)
                mm.then_inc(pv_full, 1)

            def turn_branch(c0, n0, free):
                for c in range(4):
                    pe.wait_ge(*free(c))
                    for b in range(NB):
                        mm = turn(bank[4 + c][:, b * P:b * P + P], tok[:, b, c0 + c * P:c0 + c * P + P])
                    mm.then_inc(branch_turned, 1)

            pe.wait_ge(ident_in, 16)
            for b in range(NB):
                pe.wait_ge(x_in[b], 16)
                for c in range(DC - 1):
                    mm = turn(bank[c][:, b * P:b * P + P], x_tok[:, b, c * P:c * P + P])
                    if b == NB - 1:
                        mm.then_inc(x_turned, 1)
                if b == 2:
                    pe.wait_ge(params_in, 16 * 5)
                    pe.transpose(bank[7][:, 0:R_ALL], blk[0:R_ALL, 0:P], cst[0:R_ALL, C_ID:C_ID + R_ALL]).then_inc(params_turned, 1)
            pe.wait_ge(params_ready, 1)
            for b in range(NB):
                mm = turn(bank[DC - 1][:, b * P:b * P + P], x_tok[:, b, D - P:D])
            mm.then_inc(x_turned, 1)

            with pe.Fori(0, L) as l:
                n0 = l * UNITS
                q0 = l * (TILES // 4)

                token_group(n0, q0, 4, 2, 512, l * 16, 
                            {(3, 0): lambda: sum_squares(l * 2), (3, 2): lambda: spread(l * 2)})
                with pe.Fori(0, 3) as g:
                    token_group(n0 + g * 4 + 4, q0 + g + 1, 4, 2, 512)
                token_group(n0 + 16, q0 + 4, 2, 4, 256)

                def block_and_units(b, first):
                    B = l * NB + b
                    n = n0 + b * 4
                    qb = q0 + b + TILE_B // 4

                    def conv_unit(q, midway=None):
                        feature_unit(n + (UNIT_B + q), (UNIT_B + q) % SLOTS, qb, q, uh, ul, 8, midway=midway)

                    block_turn(B)
                    conv_unit(0)
                    block_scores(B)
                    conv_unit(1)
                    block_ret(B)
                    conv_unit(2, lambda: block_ret_out(l, b, B, first))
                    block_probs(l, b, B, first)
                    conv_unit(3)
                    block_pv(b, B, first)

                block_and_units(0, True)
                with pe.Fori(1, NB) as b:
                    block_and_units(b, False)

                def gates(n, t4, off):
                    for q in range(4):
                        feature_unit(n + q, (off + q) % SLOTS, t4, q, uh, ul, 8)

                def branch(n, t4, off, ready0=None):
                    for q in range(2):
                        for e in range(2):
                            waits = None
                            if ready0 is not None and q == 0 and e == 0:
                                waits = lambda k: (branch_ready, ready0 + k + 1)
                            feature_unit(n + q, (off + q) % SLOTS, t4, 2 * q + e, bh, bl, 4, 256, P * e, e == 0, waits)

                branch(n0 + UNIT_C, q0 + TILE_C // 4, UNIT_C, l * 12)
                turn_branch(AQ, l * 8, lambda c: (pv_taken, l * NB + (NB + 1)))
                gates(n0 + (UNIT_C + 2), q0 + (TILE_C // 4 + 1), UNIT_C + 2)
                branch(n0 + (UNIT_C + 6), q0 + (TILE_C // 4 + 2), UNIT_C + 6)
                pe.wait_ge(ret_gated, l + 1)
                turn_branch(RQ, l * 8 + 4, lambda c: (branch_taken, l * 8 + c + 1))
                with pe.Fori(0, 2) as i:
                    for g in range(2):
                        o = UNIT_M + 6 * g
                        gates(n0 + i * 12 + o, q0 + i * 4 + (TILE_M // 4 + 2 * g), o)
                        branch(n0 + i * 12 + (o + 4), q0 + i * 4 + (TILE_M // 4 + 2 * g + 1), o + 4,
                               l * 12 + i * 4 + 4 if g == 0 else None)
                with pe.Fori(0, 2) as i:
                    for q in range(4):
                        waits = (lambda k: (ml_ready, l * 8 + (k + 1))) if q == 0 else None
                        feature_unit(n0 + i * 4 + (UNIT_O + q), (UNIT_O + q) % SLOTS, q0 + i + TILE_O // 4, q, mh, ml, 8,
                                     waits=waits)

                def ffn_unit(i, q, waits=None):
                    feature_unit(n0 + i * 4 + (UNIT_G + q), (UNIT_G + q) % SLOTS, q0 + i + TILE_G // 4, q, uh, ul, 8,
                                 waits=waits)

                ffn_unit(0, 0, lambda k: (u_ready, l * 16 + (8 + k + 1)))
                sum_squares(l * 2 + 1)
                ffn_unit(0, 1)
                spread(l * 2 + 1)
                ffn_unit(0, 2)
                ffn_unit(0, 3)
                with pe.Fori(1, FC // 2) as i:
                    for q in range(4):
                        ffn_unit(i, q)

                for half in range(2):
                    u0 = UNIT_D + 11 * half
                    t4 = q0 + (TILE_D // 4 + half)

                    def down(j, n, off, start=False, last=False):
                        slot = off % SLOTS
                        begin(n0 + n)
                        a = wh[:, slot, :].rearrange("p (k n) -> p k n", k=2)
                        r = wl[:, slot, :].rearrange("p (k n) -> p k n", k=2)
                        order = [(kk, c) for kk in range(2) for c in range(4)]
                        if last:
                            order = [(kk, c) for c in range(4) for kk in range(2)]
                        for at, (kk, c) in enumerate(order):
                            if half == 0:
                                pe.wait_ge(f_ready, l * FC + j * 2 + (kk + 1))
                            if start and kk == 0:
                                may_write(t4, c)
                            xh, xl = fh[:, ds(j * 2 + kk, 1), :], fl[:, ds(j * 2 + kk, 1), :]
                            xh, xl = (v.rearrange("p a t -> p (a t)") for v in (xh, xl))
                            cols = slice(c * P, c * P + P)
                            mm = pe.matmul(bank[c][:], a[:, kk, cols], xh, start=start and kk == 0, stop=False)
                            if at == 0:
                                mm.then_inc(units_begun, 1)
                            pe.matmul(bank[c][:], a[:, kk, cols], xl, start=False, stop=False)
                            mm = pe.matmul(bank[c][:], r[:, kk, cols], xh, start=False, stop=last and kk == 1)
                            if last and kk == 1:
                                mm.then_inc(tile_full, 1)

                    down(0, u0, u0, start=True)
                    with pe.Fori(0, 2) as i:
                        for q in range(4):
                            down(i * 4 + (1 + q), i * 4 + (u0 + 1 + q), u0 + 1 + q)
                    down(9, u0 + 9, u0 + 9)
                    down(10, u0 + 10, u0 + 10, last=True)

            pe.wait_ge(identr_ready, 1)
            def leave(half, b, c, o):
                t = slice(b * P, b * P + P)
                pe.wait_ge(u_ready, 2 * L * DC + 4 * half + c + 1)
                pe.matmul(o[:, c * P:c * P + P], uh[:, 4 * half + c, t], ident_r[:], start=True, stop=False)
                return pe.matmul(o[:, c * P:c * P + P], ul[:, 4 * half + c, t], ident_r[:], start=False, stop=True)

            for b in range(NB):
                for c in range(4):
                    mm = leave(0, b, c, bank[4 + b])
                mm.then_inc(out_turned, 1)
            for c in range(2):
                for b in range(NB):
                    if c == 0:
                        may_write(L * (TILES // 4), b)
                    leave(1, b, c, bank[b])
            sum_squares(2 * L, 0, 3 * P)
            for b in range(1, NB):
                leave(1, b, 2, bank[b])
            for b in (1, 2, 3, 0):
                if b == 0:
                    pe.wait_ge(std_ready, 2 * L + 1)
                    leave(1, b, 2, bank[b])
                leave(1, b, 3, bank[b]).then_inc(out_turned, 1)

        @block.scalar
        def _(act):
            for r0, src in ((R_MIX, norm_mix.rearrange("l (c p) -> (l c) p", p=P)),
                            (R_MIX + L * DC, norm_final.rearrange("(c p) -> c p", p=P)),
                            (R_FFN, norm_ffn.rearrange("l (c p) -> (l c) p", p=P)),
                            (R_BG, b_gate.rearrange("l i (c p) -> (l i c) p", p=P))):
                act.dma_start(blk[r0:r0 + src.shape[0], 0:P], src).then_inc(params_in, 16)
            act.dma_start(sinks[:], attn_sinks.rearrange("(a l) h -> a (l h)", a=1).broadcast_to([P, L * HQ])).then_inc(consts_in, 16)
            act.dma_start(x_tok[:, NB - 1, :], x.rearrange("a (b p) d -> p (a b) d", p=P)[:, NB - 1, :]).then_inc(x_in[NB - 1], 16)
            act.dma_start(cst[:, P:], consts[:, P:]).then_inc(consts_in, 16)

            def copy(dst, src, scale=1.0):
                return act.activation(dst, src, ACT.Copy, scale=scale)

            def row(buf, c):
                return buf[:, ds(c, 1), :].rearrange("p a t -> p (a t)")

            def round_h(i8, c, gain, par):
                act.wait_ge(ssq_added, i8 + 1)
                copy(row(uh, c), row(h, c), prm[:, ds(gain, 1)]).then_inc(uh_ready, 1)
                act.activation(sq[:, par, :], row(h, c), ACT.Square).then_inc(sq_ready, 1)

            def root(i, bk=4, c0=0):
                act.wait_ge(ms_ready, i + 1)
                act.activation(rms[:], bank[bk][:, c0:c0 + NB], ACT.Sqrt, bias=epsc[:], scale=1.0 / D).then_inc(std_ready, 1)

            def take_spread(i):
                act.wait_ge(rs_turned, i + 1)
                copy(rsF[:], bank[5][:]).then_inc(rsF_ready, 1)

            act.wait_ge(params_turned, 1)
            copy(prm[:], bank[7][:, 0:R_ALL]).then_inc(params_ready, 1)
            act.drain()
            for c in range(DC):
                gain = prm[:, R_MIX + c:R_MIX + c + 1]
                if c < 4:
                    act.wait_ge(bank_free[c], 1)
                    copy(uh[:, c, :], h[:, c, :], gain).then_inc(uh_ready, 1)
                else:
                    act.wait_ge(x_turned, c + 1)
                    copy(uh[:, c, :], bank[c][:], gain).then_inc(uh_ready, 1)
                    copy(h[:, c, :], bank[c][:]).then_inc(h_loaded, 1)
            act.drain()
            for c in range(DC):
                act.wait_ge(ssq_added, c + 1)
                act.activation(sq[:, c % 2, :], h[:, c, :], ACT.Square).then_inc(sq_ready, 1)

            with act.Fori(0, L) as l:
                t0 = l * TILES
                q0 = l * (TILES // 4)
                root(l * 2)
                take_spread(l * 2)
                act.wait_ge(rs_ready, l * 2 + 1)
                with act.Fori(0, 4) as g:
                    for b in range(NB):
                        full(act, t0 + g * 4 + b)
                        copy(tokf[:, ds(g * 512 + b * TOKW, 512)], bank[b][:], rs[:, b:b + 1]).then_inc(bank_free[b], 1)
                for b in range(NB):
                    full(act, t0 + (16 + b))
                    copy(tok[:, b, 2048:TOKW], bank[b][:, 0:256], rs[:, b:b + 1]).then_inc(bank_free[b], 1)

                with act.Fori(0, NB) as b:
                    B = l * NB + b
                    t = t0 + b * 4 + TILE_B
                    act.wait_ge(turned_qk, B * 3 + 1)
                    for par in range(2):
                        half = slice(64 * par, 64 * par + 64)
                        ins = copy(qs[half, par, :, :], bank[4][half, :].rearrange("p (a t) -> p a t", a=4))
                    ins.then_inc(taken_qk, 1)
                    for part in range(2):
                        copy(kwin[:, part, :, 0:P], kwin[:, part, :, P:2 * P])
                    act.wait_ge(turned_qk, B * 3 + 2)
                    for par in range(2):
                        half = slice(64 * par, 64 * par + 64)
                        copy(qpad[half, :, par, :], bank[5][half, 0:256].rearrange("p (a t) -> p a t", a=2))
                    copy(rkT[:], bank[5][:, 256:512].rearrange("p (a t) -> p a t", a=2)).then_inc(taken_qk, 1)
                    act.drain()
                    act.wait_ge(turned_qk, B * 3 + 3)
                    copy(kwin[:, 0, :, P:2 * P], bank[6][:, 0:256].rearrange("p (a t) -> p a t", a=2)).then_inc(taken_qk, 1)
                    full(act, t)
                    act.wait_ge(pv_taken, B + 1)
                    copy(ccs[:], bank[0][:]).then_inc(bank_free[0], 1)
                    act.wait_ge(max_ready, B + 1)
                    for s in range(8):
                        act.activation(S_sb[:, s, :], S_sb[:, s, :], ACT.Exp, bias=negm[:, s:s + 1],
                                       accum_out=sums[:, s:s + 1]).then_inc(exp_done, 1)
                    act.activation(sinkm[:], sinkm[:], ACT.Exp).then_inc(exp_done, 1)
                    act.wait_ge(y_full, B + 1)
                    for hd in range(RH):
                        act.activation(prod[:, hd * P:hd * P + P], bank[4][:, hd * P:hd * P + P], ACT.Square,
                                       accum_out=ssqR[:, ds(b * RH + hd, 1)])
                    copy(tcols(b, RQ, 512), bank[4][:]).then_inc(y_taken, 1)
                    full(act, t + 2)
                    copy(cbs[:], bank[2][:]).then_inc(bank_free[2], 1)
                    act.wait_ge(probs_turned, B * 4 + 1)
                    copy(PT[:, 0, :, :], bank[7][:].rearrange("p (a t) -> p a t", a=4)).then_inc(probs_a, 1)
                    act.wait_ge(probs_turned, B * 4 + 3)
                    copy(PT[:, 2, :, :], bank[6][:].rearrange("p (a t) -> p a t", a=4)).then_inc(probs_a, 1)
                    act.wait_ge(conv_ready, B + 1)
                    copy(row(bh, b), ccs[:]).then_inc(hi_ready, 1)

                act.drain()
                act.activation(rstdR[:], ssqR[:], ACT.Sqrt, bias=epsc[:], scale=1.0 / RDV).then_inc(ret_std, 1)
                act.wait_ge(bank_free[3], q0 + (TILE_B // 4 + 5))

                def gate(q, chunk_):
                    act.activation(sg[:, q, :], sg[:, q, :], ACT.Sigmoid,
                                   bias=prm[:, ds(l * 24 + (R_BG + chunk_), 1)]).then_inc(gate_ready, 1)

                def gates(g4, i, g):
                    for q in range(4):
                        act.wait_ge(bank_free[q], g4 + 2)
                        gate(q, 8 * i + 4 * g + q)

                for q in range(4):
                    gate(q, 16 + q)
                for c in range(4):
                    act.wait_ge(branch_turned, l * 8 + (c + 1))
                    copy(yfm[:, 0, c, :], bank[4 + c][:]).then_inc(branch_taken, 1)
                act.wait_ge(ret_g, l + 1)
                act.activation(tok[:, :, RG:TOKW], tok[:, :, RG:TOKW], ACT.Sigmoid).then_inc(ret_sig, 1)
                gates(q0 + (TILE_C // 4 + 1), 2, 1)
                for c in range(4):
                    act.wait_ge(branch_turned, l * 8 + (c + 5))
                    copy(yfm[:, 1, c, :], bank[4 + c][:]).then_inc(branch_taken, 1)
                act.drain()
                for i in range(2):
                    full(act, t0 + (TILE_M - 1 + 16 * i))
                    for c in range(4):
                        copy(bh[:, c, :], yfm[:, i, c, :]).then_inc(hi_ready, 1)
                    for g in range(2):
                        gates(q0 + (TILE_M // 4 + 4 * i + 2 * g), i, g)
                        if i:
                            for c in range(4 * g, 4 * g + 4):
                                act.wait_ge(m_ready, l * 16 + (8 + c + 1))
                                copy(mh[:, c, :], m[:, c, :]).then_inc(mh_ready, 1)
                with act.Fori(0, 2) as i:
                    for q in range(4):
                        act.wait_ge(bank_free[q], q0 + i + (TILE_O // 4 + 2))
                        round_h(l * 16 + i * 4 + (8 + q), i * 4 + q, l * DC + i * 4 + (R_FFN + q), q % 2)
                root(l * 2 + 1)
                take_spread(l * 2 + 1)
                with act.Fori(0, FC // 2) as i:
                    for q in range(2):
                        act.wait_ge(bank_free[2 * q], q0 + i + (TILE_G // 4 + 2))
                        act.activation(sgt[:], gp[:], ACT.Sigmoid).then_inc(sig_ready, 1)
                        act.wait_ge(f_raw, l * FC + i * 2 + (q + 1))
                        copy(row(fh, i * 2 + q), ft[:]).then_inc(fh_ready, 1)
                with act.Fori(0, 2) as i:
                    for q in range(4):
                        act.wait_ge(bank_free[q], q0 + i + (TILE_D // 4 + 2))
                        round_h(l * 16 + i * 4 + (16 + q), i * 4 + q, l * DC + i * 4 + (R_MIX + DC + q), q % 2)

            root(2 * L, 0, 3 * P)
            act.wait_ge(rs_ready, 2 * L + 1)
            for n, (half, b) in enumerate(LEAVES):
                if n % 2:
                    act.wait_ge(out_turned, n + 1)
                    copy(y_tok[:, b, 512 * half:512 * half + 512], bank[b if half else 4 + b][:],
                         rs[:, b:b + 1]).then_inc(out_ready[1], 1)

        @block.vector
        def _(dve):
            def tt(o, a, b_, op):
                return dve.tensor_tensor(o, a, b_, op)

            def row(buf, c):
                return buf[:, ds(c, 1), :].rearrange("p a t -> p (a t)")

            dve.memset(ones[:], 1.0).then_inc(split_done, SLOTS)
            dve.memset(epsc[:], EPS).then_inc(units_begun, SLOTS - 1)
            dve.memset(rs[:], 0.0).then_inc(ssq_added, 2)
            dve.memset(ssq[:], 0.0).then_inc(pv_taken, 1)
            dve.wait_ge(ident_in, 16)
            dve.tensor_copy(ident_r[:], cst[:, 0:P]).then_inc(identr_ready, 1)

            def low_h(i8, c, gain):
                dve.wait_ge(uh_ready, i8 + 1)
                dve.scalar_tensor_tensor(row(ul, c), row(h, c), prm[:, ds(gain, 1)], row(uh, c).bitcast(F32),
                                         ALU.mult, ALU.subtract).then_inc(u_ready, 1)

            def add_square(i8, par):
                dve.wait_ge(sq_ready, i8 + 1)
                tt(ssq[:], ssq[:], sq[:, par, :], ALU.add).then_inc(ssq_added, 1)
                dve.drain()

            for c in range(4):
                dve.wait_ge(x_turned, c + 1)
                dve.tensor_copy(h[:, c, :], bank[c][:]).then_inc(bank_free[c], 1)
                if c:
                    low_h(c - 1, c - 1, R_MIX + c - 1)
            low_h(3, 3, R_MIX + 3)
            for c in range(4, DC):
                dve.wait_ge(h_loaded, c - 3)
                low_h(c, c, R_MIX + c)
            for c in range(DC):
                add_square(c, c % 2)
            dve.wait_ge(consts_in, 32)

            def inverse(i):
                dve.wait_ge(std_ready, i + 1)
                dve.reciprocal(rs[:], rms[:]).then_inc(rs_ready, 1)

            def inverse_spread(i):
                inverse(i)
                dve.drain()
                dve.tensor_copy(rb[:], rs[:].unsqueeze(2).broadcast_to([P, NB, P])).then_inc(rb_ready, 1)
                dve.wait_ge(rsF_ready, i + 1)
                dve.memset(ssq[:], 0.0)

            def rope_turn(b):
                xa = tcols(b, AQ, 640).rearrange("p (h x) -> p h x", x=DH)[:, :, 0:ROT].rearrange("p h (t x) -> p h t x", t=2)
                xr = tcols(b, RQ, 512).rearrange("p (h t x) -> p h t x", t=2, x=32)
                ta = tmp[:, 0:160].rearrange("p (h t x) -> p h t x", t=2, x=8)
                tr = tmp[:, 160:672].rearrange("p (h t x) -> p h t x", t=2, x=32)

                def table(c0, half, heads):
                    return cst[:, ds(b * half + c0, half)].unsqueeze(1).unsqueeze(1).broadcast_to([P, heads, 2, half])

                tt(ta, xa, table(C_SINA, 8, 10), ALU.mult)
                tt(tr, xr, table(C_SINR, 32, 8), ALU.mult)
                dve.drain()
                tt(xa, xa, table(C_COSA, 8, 10), ALU.mult)
                tt(xr, xr, table(C_COSR, 32, 8), ALU.mult)
                dve.drain()
                for x_, t_ in ((xa, ta), (xr, tr)):
                    tt(x_[:, :, 0, :], x_[:, :, 0, :], t_[:, :, 1, :], ALU.subtract)
                    tt(x_[:, :, 1, :], x_[:, :, 1, :], t_[:, :, 0, :], ALU.add)
                dve.drain()

            def rope_place(b):
                dve.tensor_copy(blk[:, 0:512], tcols(b, AQ, 512))
                dve.tensor_copy(blk[:, 768:1280], tcols(b, RQ, 512))
                dve.tensor_copy(blk[:, 1536:2048], tcols(b, RV, 512))
                dve.tensor_copy(blk[:, 512:768].rearrange("p (g r x) -> p g r x", g=2, r=2),
                                tcols(b, AK, 128).rearrange("p (g x) -> p g x", g=2).unsqueeze(2).broadcast_to([P, 2, 2, DH]))
                tt(blk[:, 1280:1536].rearrange("p (h x) -> p h x", h=RH), tcols(b, RK, 256).rearrange("p (h x) -> p h x", h=RH),
                   cst[:, C_ZETA:C_ZETA + RH].unsqueeze(2).broadcast_to([P, RH, RDK]), ALU.mult).then_inc(rope_done, 1)

            def block_step(l, b, q0, more):
                B = l * NB + b
                t = l * TILES + b * 4 + TILE_B
                dve.wait_ge(taken_qk, B * 3 + 1)
                for par in range(2):
                    own, other = (slice(64 * p_, 64 * p_ + 64) for p_ in (par, 1 - par))
                    tt(qs[other, par, :, :], bank[4][own, :].rearrange("p (a t) -> p a t", a=4),
                       qs[own, par, :, :].bitcast(F32), ALU.subtract)
                dve.wait_ge(taken_qk, B * 3 + 2)
                tt(qx[:], bank[5][:, 0:256].rearrange("p (a t) -> p a t", a=2),
                   cst[:, C_XI:C_XI + 256].rearrange("p (a t) -> p a t", a=2), ALU.mult)
                dve.wait_ge(taken_qk, B * 3 + 3)
                tt(kwin[:, 1, :, P:2 * P], bank[6][:, 0:256].rearrange("p (a t) -> p a t", a=2),
                   kwin[:, 0, :, P:2 * P].bitcast(F32), ALU.subtract).then_inc(qx_ready, 1)
                mask = cst[:, ds(b * 256 + C_MASK, 256)].unsqueeze(1).broadcast_to([P, 2, 256])
                for n, i in enumerate((0, 2, 1, 3)):
                    dve.wait_ge(scores_full, B * 4 + (n + 1))
                    dve.scalar_tensor_tensor(S_sb[:, 2 * i:2 * i + 2, :], bank[4 + i][:].rearrange("p (a t) -> p a t", a=2),
                                             DH ** -0.5, mask, ALU.mult, ALU.add).then_inc(scores_taken, 1)
                dve.drain()
                dve.reduce_max(mx[:], S_sb[:], AXIS_X)
                dve.drain()
                sink = sinks[:, ds(l * HQ, HQ)].rearrange("p (a r) -> p r a", r=2)
                as2 = lambda v: v[:].rearrange("p (r a) -> p r a", r=2)
                tt(as2(mx), as2(mx), sink, ALU.max)
                dve.drain()
                dve.tensor_scalar(negm[:], mx[:], -1.0, None, ALU.mult)
                tt(as2(sinkm), sink, as2(mx), ALU.subtract).then_inc(max_ready, 1)
                dve.wait_ge(ret_full, B * 2 + 1)
                tt(att[:], bank[7][:].rearrange("p (a t) -> p a t", a=RH),
                   cst[:, C_DMASK:C_DMASK + 512].rearrange("p (a t) -> p a t", a=RH), ALU.mult).then_inc(att_ready, 1)
                dve.wait_ge(bank_free[0], q0 + b + (TILE_B // 4 + 2))
                tt(ccs[:], ccs[:], rs2F[:], ALU.mult)
                dve.drain()
                full(dve, t + 1)
                tt(ub[:, 2:S + 2], bank[1][:], ccs[:], ALU.mult).then_inc(bank_free[1], 1)
                dve.drain()
                w = lambda i: prm[:, ds(l * 12 + b + (R_CONV + 4 * i), 1)]
                dve.tensor_scalar(ccs[:], ub[:, 0:S], w(0), None, ALU.mult)
                dve.drain()
                for i in (1, 2):
                    dve.scalar_tensor_tensor(ccs[:], ub[:, i:S + i], w(i), ccs[:], ALU.mult, ALU.add)
                    dve.drain()
                dve.wait_ge(ret_full, B * 2 + 2)
                dve.wait_ge(y_full, B + 1)
                for hd in range(RH):
                    par, j = hd % 2, hd // 2
                    half = slice(64 * par, 64 * par + 64)
                    ins = dve.scalar_tensor_tensor(state[half, hd, :], state[half, hd, :], cst[half, C_DECAY + j:C_DECAY + j + 1],
                                                   bank[6][half, hd * P:hd * P + P], ALU.mult, ALU.add)
                ins.then_inc(state_ready, 1)
                if more:
                    rope_turn(b + 1)
                for n, bk in ((2, 5), (4, 4)):
                    dve.wait_ge(probs_turned, B * 4 + n)
                    dve.tensor_copy(PT[:, n - 1, :, :], bank[bk][:].rearrange("p (a t) -> p a t", a=4)).then_inc(probs_v, 1)
                if more:
                    rope_place(b + 1)
                dve.wait_ge(bank_free[2], q0 + b + (TILE_B // 4 + 2))
                tt(ccs[:], ccs[:], cbs[:], ALU.mult)
                dve.drain()
                tt(ccs[:], ccs[:], rsF[:], ALU.mult).then_inc(conv_ready, 1)
                dve.wait_ge(exp_done, B * 9 + 9)
                tt(rden[:], sums[:], sinkm[:], ALU.add)
                dve.drain()
                dve.reciprocal(rden[:], rden[:])
                full(dve, t + 3)
                tt(row(sg, b), bank[3][:], rsF[:], ALU.mult).then_inc(bank_free[3], 1)
                dve.wait_ge(hi_ready, l * 12 + b + 1)
                tt(row(bl, b), ccs[:], row(bh, b).bitcast(F32), ALU.subtract).then_inc(branch_ready, 1)
                dve.drain()
                dve.wait_ge(pv_full, B + 1)
                dve.tensor_copy(vprev[:], tcols(b, AV, P))
                tt(tcols(b, AQ, 512).rearrange("p (a r x) -> p r a x", r=2, x=DH),
                   bank[7][:].rearrange("p (a r x) -> p r a x", r=2, x=DH),
                   as2(rden).unsqueeze(3).broadcast_to([P, 2, 4, DH]), ALU.mult).then_inc(pv_taken, 1)

            with dve.Fori(0, L) as l:
                t0 = l * TILES
                q0 = l * (TILES // 4)
                inverse_spread(l * 2)
                tt(rs2F[:], rsF[:], rsF[:], ALU.mult)
                dve.memset(kwin[:].bitcast(F32), 0.0)
                dve.memset(vprev[:], 0.0)
                dve.memset(ub[:, 0:2], 0.0)
                dve.memset(qpad[:], 0.0)
                dve.memset(state[:], 0.0).then_inc(state_ready, 1)
                for b in range(4):
                    dve.wait_ge(bank_free[b], q0 + (TILE_A // 4 + 5))
                rope_turn(0)
                rope_place(0)
                with dve.Fori(0, NB - 1) as b:
                    block_step(l, b, q0, True)
                block_step(l, NB - 1, q0, False)

                def gate_logits(t):
                    for q in range(4):
                        full(dve, t + q)
                        tt(sg[:, q, :], bank[q][:], rsF[:], ALU.mult).then_inc(bank_free[q], 1)

                def gated(o, q, ready, t):
                    dve.wait_ge(gate_ready, l * 24 + (ready + q + 1))
                    full(dve, t + q)
                    return tt(o, sg[:, q, :], bank[q][:], ALU.mult).then_inc(bank_free[q], 1)

                for q in range(4):
                    gated(m[:, q, :], q, 0, t0 + TILE_C)
                rt = tok[:, :, RQ:RQ + 512]
                gt = tok[:, :, RG:TOKW]
                dve.wait_ge(ret_std, l + 1)
                dve.reciprocal(ssqR[:], rstdR[:])
                dve.wait_ge(y_taken, l * NB + NB)
                tt(rt, rt, gt, ALU.mult).then_inc(ret_g, 1)
                dve.drain()
                dve.wait_ge(ret_sig, l + 1)
                for b in range(NB):
                    for hd in range(RH):
                        c = slice(hd * P, hd * P + P)
                        ins = dve.scalar_tensor_tensor(rt[:, b, c], rt[:, b, c], ssqR[:, b * RH + hd:b * RH + hd + 1],
                                                       gt[:, b, c], ALU.mult, ALU.mult)
                ins.then_inc(ret_gated, 1)
                gate_logits(t0 + (TILE_C + 4))
                for q in range(4):
                    gated(m[:, 4 + q, :], q, 4, t0 + (TILE_C + 8))
                dve.drain()
                for i in range(2):
                    for c in range(4):
                        dve.wait_ge(hi_ready, l * 12 + (4 * i + 5 + c))
                        tt(bl[:, c, :], yfm[:, i, c, :], bh[:, c, :].bitcast(F32), ALU.subtract).then_inc(branch_ready, 1)
                    for g in range(2):
                        t = t0 + (TILE_M + 16 * i + 8 * g)
                        gate_logits(t)

                        def low_m(c):
                            dve.wait_ge(mh_ready, l * 8 + (c + 1))
                            tt(ml[:, c, :], m[:, c, :], mh[:, c, :].bitcast(F32), ALU.subtract).then_inc(ml_ready, 1)

                        for q in range(4):
                            gated(prod[:], q, 8 + 8 * i + 4 * g, t + 4)
                            dve.drain()
                            tt(m[:, 4 * g + q, :], m[:, 4 * g + q, :], prod[:], ALU.add).then_inc(m_ready, 1)
                            if i and q:
                                low_m(4 * g + q - 1)
                            dve.drain()
                        if i:
                            low_m(4 * g + 3)

                def into_h(i8, t, c, gain, squares_first=False):
                    def add(q):
                        full(dve, t + q)
                        tt(row(h, c + q), row(h, c + q), bank[q][:], ALU.add).then_inc(bank_free[q], 1)

                    def low(q):
                        low_h(i8 + q, c + q, gain + q)

                    def square(q):
                        add_square(i8 + q, q % 2)

                    add(0)
                    add(1)
                    low(0)
                    square(0)
                    add(2)
                    low(1)
                    add(3)
                    square(1)
                    low(2)
                    square(2)
                    for step in (square, low) if squares_first else (low, square):
                        step(3)

                dve.drain()
                dve.memset(ssq[:], 0.0)
                dve.drain()
                with dve.Fori(0, 2) as i:
                    into_h(l * 16 + i * 4 + 8, t0 + i * 4 + TILE_O, i * 4, l * DC + i * 4 + R_FFN)
                inverse_spread(l * 2 + 1)
                with dve.Fori(0, FC // 2) as i:
                    t = t0 + i * 4 + TILE_G
                    for q in range(2):
                        full(dve, t + 2 * q)
                        tt(gp[:], bank[2 * q][:], rsF[:], ALU.mult).then_inc(bank_free[2 * q], 1)
                        full(dve, t + (2 * q + 1))
                        tt(ft[:], bank[2 * q + 1][:], rsF[:], ALU.mult).then_inc(bank_free[2 * q + 1], 1)
                        dve.wait_ge(sig_ready, l * FC + i * 2 + (q + 1))
                        tt(gp[:], gp[:], sgt[:], ALU.mult)
                        dve.drain()
                        tt(ft[:], gp[:], ft[:], ALU.mult).then_inc(f_raw, 1)
                        dve.wait_ge(fh_ready, l * FC + i * 2 + (q + 1))
                        tt(row(fl, i * 2 + q), ft[:], row(fh, i * 2 + q).bitcast(F32), ALU.subtract).then_inc(f_ready, 1)
                        dve.drain()
                with dve.Fori(0, 2) as i:
                    into_h(l * 16 + i * 4 + 16, t0 + i * 4 + TILE_D, i * 4, l * DC + i * 4 + (R_MIX + DC), True)

            inverse(2 * L)
            dve.drain()
            for n, (half, b) in enumerate(LEAVES):
                if n % 2 == 0:
                    dve.wait_ge(out_turned, n + 1)
                    dve.tensor_scalar(y_tok[:, b, 512 * half:512 * half + 512], bank[b if half else 4 + b][:],
                                      rs[:, b:b + 1], None, ALU.mult).then_inc(out_ready[0], 1)


_INS = ["x", "norm_mix", "w_in", "attn_sinks", "conv_w", "w_branch", "b_gate", "w_out",
        "norm_ffn", "w_ffn_gate", "w_ffn_up", "w_ffn_down", "norm_final"]


def kernel(**inputs):
    import concourse.bacc as bacc
    from concourse.bass_utils import run_bass_kernel_spmd

    arrays = {name: np.ascontiguousarray(inputs[name]) for name in _INS}
    arrays["consts"] = shape_constants(arrays["x"].shape[1])
    nc = bacc.Bacc("TRN2", target_bir_lowering=False, num_devices=1, dynamic_dma_scratch_size=1024)
    args = [nc.dram_tensor(n, a.shape, mybir.dt.from_np(a.dtype), kind="ExternalInput").ap() for n, a in arrays.items()]
    out = nc.dram_tensor("out", arrays["x"].shape, F32, kind="ExternalOutput").ap()
    trunk(nc, *args, out)
    return run_bass_kernel_spmd(nc, [arrays], core_ids=[0]).results[0]["out"]
```
